# Optimizing a Trainium2 kernel written in Bass

```python
import jax
import jax.numpy as jnp
from jax import lax
import numpy as np

D_MODEL = 1024
BATCH = 1
SEQ = 256
DEPTH = 2

HEAD_DIM = 64
DIL_PATTERNS = ((128, 1), (512, 4), (2048, 16))
DIL_HEADS_PER_GROUP = 4
DIL_HEADS = len(DIL_PATTERNS) * DIL_HEADS_PER_GROUP
DIL_QBLOCK = 64
NA_HEADS = 8
GRID_W = 64
NA_ROWS_MAX = 8
NA_COLS = 16
NA_QCOLS = 16
D_FF = 2816
ROPE_THETA = 10000.0
RMS_EPS = 1e-6
NEG_INF = -1e30
DIL_QKV = 3 * DIL_HEADS * HEAD_DIM
NA_QKV = 3 * NA_HEADS * HEAD_DIM
IN_WIDTH = DIL_QKV + NA_QKV + 2 * D_MODEL

kernel_name = 'hybrid_dilated_neighbourhood_macaron'

def rms_norm(x, g):
    x32 = x.astype(jnp.float32)
    y = x32 * lax.rsqrt(jnp.mean(x32 * x32, axis=-1, keepdims=True) + RMS_EPS)
    return (y * g.astype(jnp.float32)).astype(x.dtype)

def swiglu(x, w_up, w_down):
    gate, up = jnp.split(x @ w_up, 2, axis=-1)
    return (jax.nn.silu(gate) * up) @ w_down

def rotary(t, pos):
    half = HEAD_DIM // 2
    inv_freq = ROPE_THETA ** (-jnp.arange(half, dtype=jnp.float32) / half)
    ang = pos.astype(jnp.float32)[:, None] * inv_freq[None, :]
    cos = jnp.cos(ang).astype(t.dtype)
    sin = jnp.sin(ang).astype(t.dtype)
    t1, t2 = t[..., :half], t[..., half:]
    return jnp.concatenate([t1 * cos - t2 * sin, t2 * cos + t1 * sin], axis=-1)

def dilated_window_attention(q, k, v, dilation, half):
    b, g, s, hd = q.shape
    sub_len = s // dilation
    bq = min(DIL_QBLOCK, sub_len)
    nb = -(-sub_len // bq)
    padded = nb * bq
    nk = bq + 2 * half

    def to_sub(t):
        return t.reshape(b, g, sub_len, dilation, hd).transpose(0, 1, 3, 2, 4)

    qs = jnp.pad(to_sub(q), ((0, 0), (0, 0), (0, 0), (0, padded - sub_len), (0, 0)))
    qs = qs.reshape(b, g, dilation, nb, bq, hd)
    key_idx = np.arange(nb)[:, None] * bq + np.arange(nk)[None, :]
    kpad = ((0, 0), (0, 0), (0, 0), (half, padded - sub_len + half), (0, 0))
    ks = jnp.pad(to_sub(k), kpad)[:, :, :, key_idx]
    vs = jnp.pad(to_sub(v), kpad)[:, :, :, key_idx]
    q_pos = np.arange(nb)[:, None] * bq + np.arange(bq)[None, :]
    k_pos = key_idx - half
    rel = k_pos[:, None, :] - q_pos[:, :, None]
    valid = (np.abs(rel) <= half) & (k_pos[:, None, :] >= 0) & (k_pos[:, None, :] < sub_len)
    scores = jnp.einsum('bgrnqd,bgrnkd->bgrnqk', qs, ks).astype(jnp.float32) * (hd ** -0.5)
    scores = jnp.where(valid, scores, NEG_INF)
    m = jnp.max(scores, axis=-1, keepdims=True)
    p = jnp.exp(scores - m)
    den = jnp.sum(p, axis=-1)
    o = jnp.einsum('bgrnqk,bgrnkd->bgrnqd', p.astype(v.dtype), vs).astype(jnp.float32) / den[..., None]
    lse = m[..., 0] + jnp.log(den)
    o = o.reshape(b, g, dilation, padded, hd)[:, :, :, :sub_len]
    o = o.transpose(0, 1, 3, 2, 4).reshape(b, g, s, hd)
    lse = lse.reshape(b, g, dilation, padded)[..., :sub_len].transpose(0, 1, 3, 2).reshape(b, g, s)
    return o, lse

def neighbourhood_attention(q, k, v, rel_bias):
    b, nh, s, hd = q.shape
    rows = s // GRID_W
    kr = min(NA_ROWS_MAX, rows)
    n_cb = GRID_W // NA_QCOLS
    kcw = 2 * NA_QCOLS
    q_cols = np.arange(GRID_W).reshape(n_cb, NA_QCOLS)
    key_cols = (np.clip(np.arange(n_cb) * NA_QCOLS - NA_QCOLS // 2, 0, GRID_W - kcw)[:, None]
                + np.arange(kcw)[None, :])
    win_lo = np.clip(q_cols - NA_COLS // 2, 0, GRID_W - NA_COLS)
    col_valid = ((key_cols[:, None, :] >= win_lo[:, :, None])
                 & (key_cols[:, None, :] < win_lo[:, :, None] + NA_COLS))
    col_idx = np.clip(key_cols[:, None, :] - q_cols[:, :, None] + NA_COLS - 1, 0, 2 * NA_COLS - 2)
    row_ids = np.arange(rows)
    row_lo = np.clip(row_ids - kr // 2, 0, rows - kr)
    row_idx = row_lo[:, None] + np.arange(kr)[None, :] - row_ids[:, None] + NA_ROWS_MAX - 1
    bias = rel_bias.astype(jnp.float32)[:, row_idx][..., col_idx]
    bias = jnp.where(col_valid[:, :, None, :], bias.transpose(1, 0, 3, 4, 2, 5), NEG_INF)
    kg = k.reshape(b, nh, rows, GRID_W, hd)
    vg = v.reshape(b, nh, rows, GRID_W, hd)
    q_rows = q.reshape(b, nh, rows, n_cb, NA_QCOLS, hd).transpose(2, 0, 1, 3, 4, 5)
    scale = hd ** -0.5

    def one_row(args):
        q_r, lo, bias_r = args
        k_r = lax.dynamic_slice_in_dim(kg, lo, kr, axis=2)[:, :, :, key_cols]
        v_r = lax.dynamic_slice_in_dim(vg, lo, kr, axis=2)[:, :, :, key_cols]
        sc = jnp.einsum('bhcqd,bhrckd->bhcqrk', q_r, k_r).astype(jnp.float32) * scale + bias_r
        p = jax.nn.softmax(sc.reshape(b, nh, n_cb, NA_QCOLS, kr * kcw), axis=-1).reshape(sc.shape)
        return jnp.einsum('bhcqrk,bhrckd->bhcqd', p.astype(v.dtype), v_r)

    out = lax.map(one_row, (q_rows, jnp.asarray(row_lo, dtype=jnp.int32), bias))
    return out.reshape(rows, b, nh, GRID_W, hd).transpose(1, 2, 0, 3, 4).reshape(b, nh, s, hd)

def hybrid_mixer(h, w_in, rel_bias, w_branch_a, w_branch_b, w_out, pos):
    b, s, _ = h.shape
    proj = h @ w_in
    a_qkv = proj[..., :DIL_QKV]
    b_qkv = proj[..., DIL_QKV:DIL_QKV + NA_QKV]
    gate_a, gate_b = jnp.split(jax.nn.sigmoid(proj[..., DIL_QKV + NA_QKV:]), 2, axis=-1)

    def heads(t, n):
        return t.reshape(b, s, n, HEAD_DIM).transpose(0, 2, 1, 3)

    qa, ka, va = (heads(t, DIL_HEADS) for t in jnp.split(a_qkv, 3, axis=-1))
    qa, ka = rotary(qa, pos), rotary(ka, pos)
    outs, lses = [], []
    for gi, (window, dilation) in enumerate(DIL_PATTERNS):
        grp = slice(gi * DIL_HEADS_PER_GROUP, (gi + 1) * DIL_HEADS_PER_GROUP)
        o, lse = dilated_window_attention(qa[:, grp], ka[:, grp], va[:, grp], dilation, (window // 2) // dilation)
        outs.append(o)
        lses.append(lse)
    mix_w = jax.nn.softmax(jnp.stack(lses), axis=0)
    ya = jnp.sum(mix_w[..., None] * jnp.stack(outs), axis=0).astype(h.dtype)
    ya = ya.transpose(0, 2, 1, 3).reshape(b, s, DIL_HEADS_PER_GROUP * HEAD_DIM)

    qb, kb, vb = (heads(t, NA_HEADS) for t in jnp.split(b_qkv, 3, axis=-1))
    yb = neighbourhood_attention(qb, kb, vb, rel_bias)
    yb = yb.transpose(0, 2, 1, 3).reshape(b, s, NA_HEADS * HEAD_DIM)

    merged = gate_a * (ya @ w_branch_a) + gate_b * (yb @ w_branch_b)
    return merged @ w_out

def setup_inputs(seed: int = 0) -> dict:
    key = jax.random.key(seed)
    ks = jax.random.split(key, 14)
    f32 = jnp.float32

    def normal(k, shape, scale):
        return jax.random.normal(k, shape, f32) * scale

    def gain(k, shape):
        return 1.0 + 0.05 * jax.random.normal(k, shape, f32)

    return {
        'x': normal(ks[0], (BATCH, SEQ, D_MODEL), 1.0),
        'ffn1_norm': gain(ks[1], (DEPTH, D_MODEL)),
        'ffn1_w_up': normal(ks[2], (DEPTH, D_MODEL, 2 * D_FF), D_MODEL ** -0.5),
        'ffn1_w_down': normal(ks[3], (DEPTH, D_FF, D_MODEL), D_FF ** -0.5),
        'mix_norm': gain(ks[4], (DEPTH, D_MODEL)),
        'w_in': normal(ks[5], (DEPTH, D_MODEL, IN_WIDTH), D_MODEL ** -0.5),
        'na_rel_bias': normal(ks[6], (DEPTH, NA_HEADS, 2 * NA_ROWS_MAX - 1, 2 * NA_COLS - 1), 0.1),
        'w_branch_a': normal(ks[7], (DEPTH, DIL_HEADS_PER_GROUP * HEAD_DIM, D_MODEL), (DIL_HEADS_PER_GROUP * HEAD_DIM) ** -0.5),
        'w_branch_b': normal(ks[8], (DEPTH, NA_HEADS * HEAD_DIM, D_MODEL), (NA_HEADS * HEAD_DIM) ** -0.5),
        'w_out': normal(ks[9], (DEPTH, D_MODEL, D_MODEL), D_MODEL ** -0.5),
        'ffn2_norm': gain(ks[10], (DEPTH, D_MODEL)),
        'ffn2_w_up': normal(ks[11], (DEPTH, D_MODEL, 2 * D_FF), D_MODEL ** -0.5),
        'ffn2_w_down': normal(ks[12], (DEPTH, D_FF, D_MODEL), D_FF ** -0.5),
        'final_norm': gain(ks[13], (D_MODEL,)),
    }

def reference(x, ffn1_norm, ffn1_w_up, ffn1_w_down, mix_norm, w_in, na_rel_bias, w_branch_a,
              w_branch_b, w_out, ffn2_norm, ffn2_w_up, ffn2_w_down, final_norm):
    pos = jnp.arange(x.shape[1])
    for l in range(DEPTH):
        x = x + 0.5 * swiglu(rms_norm(x, ffn1_norm[l]), ffn1_w_up[l], ffn1_w_down[l])
        x = x + hybrid_mixer(rms_norm(x, mix_norm[l]), w_in[l], na_rel_bias[l], w_branch_a[l],
                             w_branch_b[l], w_out[l], pos)
        x = x + 0.5 * swiglu(rms_norm(x, ffn2_norm[l]), ffn2_w_up[l], ffn2_w_down[l])
    return rms_norm(x, final_norm)


_drawn_inputs = setup_inputs


def setup_inputs(seed=0):
    import zlib

    import numpy as np

    out = dict(_drawn_inputs(seed))
    spreads = {}
    factors = {'mix_norm': 3.63, 'na_rel_bias': 3.984}
    for name, (base, spread) in spreads.items():
        noise = np.random.default_rng([zlib.crc32(name.encode()), seed]).standard_normal(out[name].shape)
        drawn = base * np.exp(spread * noise) if base else spread * noise
        out[name] = jnp.asarray(drawn.astype(out[name].dtype))
    for name, factor in factors.items():
        out[name] = (out[name] * factor).astype(out[name].dtype)
    return out
```

```python
from contextlib import ExitStack

import concourse.bass as bass
import numpy as np
from concourse import mybir

ALU = mybir.AluOpType
ACT = mybir.ActivationFunctionType
F32 = mybir.dt.float32
F32R = mybir.dt.float32r

P = 128
SEQ = 256
TT = SEQ // P
D = 1024
KT = D // P
DEPTH = 2
D_FF = 2816
HD = 64
HALF = HD // 2
DIL_PATTERNS = ((128, 1), (512, 4), (2048, 16))
GROUPS = len(DIL_PATTERNS)
GROUP_HEADS = 4
DIL_HEADS = GROUPS * GROUP_HEADS
NA_HEADS = 8
HEADS = DIL_HEADS + NA_HEADS
GRID_W = 64
NA_COLS = 16
REL_ROWS, REL_COLS = 15, 31
DIL_W = DIL_HEADS * HD
NA_W = NA_HEADS * HD
NA_AT = 3 * DIL_W
GATE_AT = NA_AT + 3 * NA_W
IN_WIDTH = GATE_AT + 2 * D
EPS = 1e-6
NEG_INF = -1e30

NB = 512
UNIT = 2048
RING = 3
FC = 256
CHUNKS = D_FF // FC
F_UNITS = 3 * CHUNKS
M_UNITS = 30
L_UNITS = 2 * F_UNITS + M_UNITS
F1_AT, M_AT, F2_AT = 0, F_UNITS, F_UNITS + M_UNITS
assert F_UNITS % RING == 0 and M_UNITS % RING == 0
PHASES = 3
PAIRS = HEADS // 2
DIL_PAIRS = DIL_HEADS // 2
BIAS_ROWS = 6

V_AT, VC_AT, NQ_AT, G_AT, BA_AT, BB_AT, O_AT = 6, 8, 9, 15, 23, 24, 26
PROJ_CHUNKS = 12
QK_CHUNKS = (0, 1, 2, 5, 6)
Y_AT = 22

C_MASK = 0
C_NAMASK = C_MASK + GROUPS * TT * SEQ
C_COS = C_NAMASK + GRID_W
C_SIN = C_COS + TT * HALF
C_IDENT = C_SIN + TT * HALF
C_ALL = C_IDENT + P


def chunk_steps(i):
    if i < 4:
        return (2 * i, 2 * i + 1)
    if i == 4:
        return (VC_AT,)
    return (NQ_AT + 2 * (i - 5), NQ_AT + 2 * (i - 5) + 1)


def step_chunk(m):
    for i in range(PROJ_CHUNKS):
        if m in chunk_steps(i):
            return i, chunk_steps(i).index(m)
    return None, 0


def pair_step(p):
    return NQ_AT + p if p < DIL_PAIRS else G_AT + 1 + p - DIL_PAIRS


def step_pair(m):
    for p in range(PAIRS):
        if pair_step(p) == m:
            return p
    return None


def build(nc, x_in, gains, w_up, w_down, w_in, rel_bias, w_a, w_b, w_out, consts, out):
    bias_rows = nc.dram_tensor("bias_rows", [DEPTH, P, NA_HEADS, BIAS_ROWS, GRID_W], F32, kind="Internal").ap()
    with ExitStack() as ctx:
        def sb(name, shape, dt=F32):
            return ctx.enter_context(nc.sbuf_tensor(name, shape, dt))

        def sem(name):
            return ctx.enter_context(nc.semaphore(name))

        raw = [sb(f"raw{i}", [P, UNIT]) for i in range(RING)]
        w_hi = [sb(f"w_hi{i}", [P, UNIT], F32R) for i in range(RING)]
        w_lo = [sb(f"w_lo{i}", [P, UNIT], F32R) for i in range(RING)]
        x = sb("x", [P, TT, D])
        gain = sb("gain", [P, D])
        a_hi = sb("a_hi", [P, KT, SEQ], F32R)
        a_lo = sb("a_lo", [P, KT, SEQ], F32R)
        qT = sb("qT", [P, PAIRS, SEQ])
        kT = sb("kT", [P, PAIRS, SEQ])
        v = sb("v", [P, TT, HEADS * HD])
        qk_raw = sb("qk_raw", [P, TT, NB])
        gates = sb("gates", [P, TT, 2 * D])
        bias = sb("bias", [P, NA_HEADS, BIAS_ROWS, GRID_W])
        cst = sb("cst", [P, C_ALL])
        hT_hi = sb("hT_hi", [P, 2, SEQ], F32R)
        hT_lo = sb("hT_lo", [P, 2, SEQ], F32R)
        probs = sb("probs", [P, 2, TT, SEQ])
        probsT = sb("probsT", [P, 2, TT, SEQ])
        o_dil = sb("o_dil", [P, DIL_HEADS, TT, HD])
        y = sb("y", [P, TT, GROUP_HEADS * HD + NA_W])
        yT_hi = sb("yT_hi", [P, 6, SEQ], F32R)
        yT_lo = sb("yT_lo", [P, 6, SEQ], F32R)
        top = sb("top", [P, HEADS, TT])
        neg_top = sb("neg_top", [P, HEADS, TT])
        den = sb("den", [P, HEADS, TT])
        rden = sb("rden", [P, 2, TT])
        mix = sb("mix", [P, 6, GROUP_HEADS * TT])
        mix_e = sb("mix_e", [P, GROUPS, GROUP_HEADS * TT])
        mix_d = sb("mix_d", [P, GROUPS, GROUP_HEADS * TT])
        stat = sb("stat", [P, 8, TT])
        wait_carrier = sb("wait_carrier", [P, 1])
        credits = sb("credits", [P, 2 * RING])

        flat_gates = gates[:, :, :].rearrange("p t n -> p (t n)")
        xg = flat_gates[:, 0:TT * D].rearrange("p (t n) -> p t n", t=TT)
        rope_tmp = flat_gates[:, 0:4 * TT * 8 * HALF].rearrange("p (i t h d) -> p i t h d", i=4, t=TT, h=8)
        qk_rot = flat_gates[:, TT * D:TT * D + TT * NB].rearrange("p (t n) -> p t n", t=TT)
        flat_probs = probs[:, :, :, :].rearrange("p a t k -> p (a t k)")
        tanh_g = flat_probs[:, 0:TT * FC].rearrange("p (t n) -> p t n", t=TT)
        gated = flat_probs[:, TT * FC:2 * TT * FC].rearrange("p (t n) -> p t n", t=TT)
        hidden = probsT[:, :, :, :].rearrange("p a t k -> p (a t k)")[:, 0:TT * FC].rearrange("p (t n) -> p t n", t=TT)
        squares = flat_probs
        merged = qT[:, :, :].rearrange("p a b -> p (a b)")[:, 0:TT * D].rearrange("p (t n) -> p t n", t=TT)
        from_b = qk_raw[:, 0, :]

        dil_mask = cst[:, C_MASK:C_NAMASK].rearrange("p (g t k) -> p g t k", g=GROUPS, t=TT)
        na_mask = cst[:, C_NAMASK:C_COS]
        cos = cst[:, C_COS:C_SIN].rearrange("p (t d) -> p t d", t=TT)
        sin = cst[:, C_SIN:C_IDENT].rearrange("p (t d) -> p t d", t=TT)
        ident = cst[:, C_IDENT:C_ALL]
        sum_sq, rstd, half_rstd, half_rstd2 = (stat[:, i, :] for i in range(4))
        minus_half, half, one_over_d, eps = (stat[:, i, :] for i in range(4, 8))

        bank = [ctx.enter_context(nc.psum_tensor(f"bank{i}", [P, NB], F32)) for i in range(8)]
        UP = (0, 1)
        TR = (2, 3)
        HT = 2
        ACC = ((4, 5), (6, 7))
        PROJ = ((0, 1), (4, 5))
        SC = (6, 7)
        PT, OB = 2, 3
        YT = (6, 7, 2)
        BANK_A = ((0, 1), (6, 7))
        BANK_B = ((4, 2), (5, 3))
        MT = (0, 1)

        x_loaded = sem("x_loaded")
        consts_loaded = sem("consts_loaded")
        gain_loaded = sem("gain_loaded")
        bias_spread = sem("bias_spread")
        bias_loaded = sem("bias_loaded")
        bias_ready = sem("bias_ready")
        raw_arrived = [sem(f"raw_arrived{i}") for i in range(RING)]
        hi_done = sem("hi_done")
        lo_done = sem("lo_done")
        split_free = sem("split_free")
        x_updated = sem("x_updated")
        xg_ready = sem("xg_ready")
        xT_done = sem("xT_done")
        xT_hi = sem("xT_hi")
        xT_lo = sem("xT_lo")
        squares_done = sem("squares_done")
        pool_chain = sem("pool_chain")
        numbers_set = sem("numbers_set")
        rstd_ready = sem("rstd_ready")
        up_done = sem("up_done")
        tanh_done = sem("tanh_done")
        gated_done = sem("gated_done")
        hidden_done = sem("hidden_done")
        hT_done = sem("hT_done")
        hT_hi_done = sem("hT_hi_done")
        hT_lo_done = sem("hT_lo_done")
        acc_done = sem("acc_done")
        proj_done = sem("proj_done")
        proj_read = sem("proj_read")
        rope_dve = sem("rope_dve")
        rope_dve_part = sem("rope_dve_part")
        rope_pool = sem("rope_pool")
        rope_pool_part = sem("rope_pool_part")
        qkT_done = sem("qkT_done")
        qkT_read = sem("qkT_read")
        scores_done = sem("scores_done")
        scores_read = sem("scores_read")
        neg_top_done = sem("neg_top_done")
        exp_done = sem("exp_done")
        probsT_done = sem("probsT_done")
        probsT_read = sem("probsT_read")
        pv_done = sem("pv_done")
        rden_done = sem("rden_done")
        o_read = sem("o_read")
        mix_chain = sem("mix_chain")
        mix_exp_in = sem("mix_exp_in")
        mix_exp = sem("mix_exp")
        mix_ready = sem("mix_ready")
        mix_part = sem("mix_part")
        y_dil_done = sem("y_dil_done")
        gates_done = sem("gates_done")
        yT_done = sem("yT_done")
        yT_hi_done = sem("yT_hi_done")
        yT_lo_done = sem("yT_lo_done")
        a_done = sem("a_done")
        a_read = sem("a_read")
        b_done = sem("b_done")
        b_read = sem("b_read")
        merged_done = sem("merged_done")
        mT_done = sem("mT_done")
        mT_hi = sem("mT_hi")
        mT_lo = sem("mT_lo")
        result_ready = sem("result_ready")
        out_written = sem("out_written")

        GROUP4 = ((0, 0), (0, 1), (1, 0), (1, 1))
        HALF_MAJOR = ((0, 0), (1, 0), (0, 1), (1, 1))

        def unit_used(eng, l, at, u, c=None):
            n = l * L_UNITS + at + u + 1 + RING
            eng.wait_ge(split_free, n if c is None else n + c * 3)

        block = ctx.enter_context(nc.Block())

        @block.sync
        def _(sp):
            def unit(n, slot, parts):
                sp.wait_ge(lo_done, n + 1)
                for dst, src in parts(raw[slot]):
                    sp.dma_start(dst, src).then_inc(raw_arrived[slot], 16)

            def load_gain(row):
                sp.dma_start(gain[:, :], gains[row, :].partition_broadcast(P)).then_inc(gain_loaded, 16)

            def up_unit(f, l, c, a):
                src = w_up[f].rearrange("l (k p) n -> l p k n", p=P)

                def parts(place):
                    to = place[:, :].rearrange("p (k n) -> p k n", n=2 * FC)
                    for g in range(2):
                        cols = src[:, :, 4 * a:4 * a + 4, g * D_FF:(g + 1) * D_FF]
                        yield to[:, :, g * FC:(g + 1) * FC], cols[l, :, :, bass.ts(c, FC)]
                return parts

            def rows_unit(w, l, k0):
                src = w.rearrange("l (k p) n -> l p k n", p=P)

                def parts(place):
                    for j in range(2):
                        yield place[:, j * D:(j + 1) * D], src[l, :, k0 + j, :]
                return parts

            def down_unit(f, l, c):
                rows = w_down[f].rearrange("l (k p) n -> l k p n", p=P)

                def parts(place):
                    for j in range(2):
                        yield place[:, j * D:(j + 1) * D], rows[l, c * 2 + j, :, :]
                return parts

            def cols_unit(l, c0, a):
                src = w_in.rearrange("l (k p) n -> l p k n", p=P)

                def parts(place):
                    to = place[:, :].rearrange("p (k n) -> p k n", n=NB)
                    for j in range(2):
                        k = 4 * a + 2 * j
                        yield to[:, 2 * j:2 * j + 2, :], src[l, :, k:k + 2, c0:c0 + NB]
                return parts

            def qk_unit(l, g, a):
                src = w_in.rearrange("l (k p) n -> l p k n", p=P)
                w = GROUP_HEADS * HD

                def parts(place):
                    to = place[:, :].rearrange("p (k n) -> p k n", n=NB)
                    for j in range(2):
                        c0 = j * DIL_W + g * w
                        yield to[:, :, j * w:(j + 1) * w], src[l, :, 4 * a:4 * a + 4, c0:c0 + w]
                return parts

            def last_v_unit(l):
                src = w_in.rearrange("l (k p) n -> l p k n", p=P)
                c0 = 2 * DIL_W + NB

                def parts(place):
                    to = place[:, :].rearrange("p (k n) -> p k n", n=DIL_W - NB)
                    for j in range(2):
                        yield to[:, 4 * j:4 * j + 4, :], src[l, :, 4 * j:4 * j + 4, c0:NA_AT]
                return parts

            def feed_forward(f, l, at, next_gain):
                n0 = l * L_UNITS + at
                unit(n0, 0, up_unit(f, l, 0, 0))
                unit(n0 + 1, 1, up_unit(f, l, 0, 1))
                with sp.Fori(1, CHUNKS) as c:
                    unit(n0 + c * 3 - 1, 2, up_unit(f, l, c, 0))
                    unit(n0 + c * 3, 0, up_unit(f, l, c, 1))
                    unit(n0 + c * 3 + 1, 1, down_unit(f, l, c - 1))
                load_gain(next_gain)
                unit(n0 + F_UNITS - 1, 2, down_unit(f, l, CHUNKS - 1))

            sp.dma_start(gain[:, :], gains[0, :].partition_broadcast(P)).then_inc(gain_loaded, 16)
            with sp.Fori(0, DEPTH) as l:
                feed_forward(0, l, F1_AT, l * PHASES + 1)
                sp.wait_ge(bias_spread, 16 * DEPTH * 2 * BIAS_ROWS)
                sp.dma_start(bias[:, :, :, :].rearrange("p h r k -> p (h r k)"),
                             bias_rows.rearrange("l p h r k -> l p (h r k)")[l, :, :]).then_inc(bias_loaded, 16)
                n0 = l * L_UNITS + M_AT
                m = 0
                for g in range(GROUPS):
                    for a in range(2):
                        unit(n0 + m, m % RING, qk_unit(l, g, a))
                        m += 1
                for a in range(2):
                    unit(n0 + m, m % RING, cols_unit(l, 2 * DIL_W, a))
                    m += 1
                unit(n0 + m, m % RING, last_v_unit(l))
                m += 1
                for i in range(7):
                    for a in range(2):
                        unit(n0 + m, m % RING, cols_unit(l, NA_AT + i * NB, a))
                        m += 1
                unit(n0 + m, m % RING, rows_unit(w_a, l, 0))
                m += 1
                load_gain(l * PHASES + 2)
                for k0 in (0, 2):
                    unit(n0 + m, m % RING, rows_unit(w_b, l, k0))
                    m += 1
                for k0 in range(0, KT, 2):
                    unit(n0 + m, m % RING, rows_unit(w_out, l, k0))
                    m += 1
                feed_forward(1, l, F2_AT, l * PHASES + 3)
            for t in range(TT):
                sp.wait_ge(result_ready, t + 1)
                sp.dma_start(out[t * P:(t + 1) * P, :], xg[:, t, :]).then_inc(out_written, 16)
            sp.wait_ge(out_written, 16 * TT)

        @block.gpsimd
        def _(pool):
            for tile, number in ((minus_half, -0.5), (half, 0.5), (one_over_d, 1.0 / D), (eps, EPS)):
                pool.memset(tile, number).then_inc(numbers_set, 1)
            for l in range(DEPTH):
                for a in range(2):
                    for r in range(BIAS_ROWS):
                        at = l * NA_HEADS * REL_ROWS * REL_COLS + (r - 2 - a + 7) * REL_COLS + NA_COLS - 1
                        src = bass.AP(rel_bias.tensor, at, [[REL_ROWS * REL_COLS, NA_HEADS], [-1, GRID_W], [1, GRID_W]])
                        dst = bias_rows[l, GRID_W * a:GRID_W * (a + 1), :, r, :].rearrange("q h k -> h q k")
                        pool.dma_start(dst, src).then_inc(bias_spread, 16)

            def norm_factors(ph):
                pool.wait_ge(squares_done, ph * TT + TT)
                pool.tensor_tensor(rstd, sum_sq, one_over_d, ALU.mult).then_inc(pool_chain, 1)
                pool.wait_ge(pool_chain, ph * 4 + 1)
                pool.tensor_tensor(rstd, rstd, eps, ALU.add).then_inc(pool_chain, 1)
                pool.wait_ge(pool_chain, ph * 4 + 2)
                pool.tensor_tensor(rstd, rstd, minus_half, ALU.pow).then_inc(pool_chain, 1)
                pool.wait_ge(pool_chain, ph * 4 + 3)
                pool.tensor_tensor(half_rstd, rstd, half, ALU.mult).then_inc(pool_chain, 1)
                pool.wait_ge(pool_chain, ph * 4 + 4)
                pool.tensor_tensor(half_rstd2, rstd, half_rstd, ALU.mult).then_inc(rstd_ready, 1)

            def rope(l, i):
                heads = qk_raw[:, :, :].rearrange("p t (h s d) -> p t h s d", h=8, s=2)
                turned = qk_rot.rearrange("p t (h s d) -> p t h s d", h=8, s=2)
                c = cos.unsqueeze(2).to_broadcast([P, TT, 8, HALF])
                s = sin.unsqueeze(2).to_broadcast([P, TT, 8, HALF])
                pool.wait_ge(proj_read, l * 16 + 2 * i + 2)
                if i >= 1:
                    pool.wait_ge(qkT_done, l * 5 + i)
                pool.tensor_tensor(rope_tmp[:, 2], heads[:, :, :, 1, :], c, ALU.mult).then_inc(rope_pool_part, 1)
                pool.tensor_tensor(rope_tmp[:, 3], heads[:, :, :, 0, :], s, ALU.mult).then_inc(rope_pool_part, 1)
                pool.wait_ge(rope_pool_part, l * 6 + 2 * i + 2)
                pool.tensor_tensor(turned[:, :, :, 1, :], rope_tmp[:, 2], rope_tmp[:, 3], ALU.add).then_inc(rope_pool, 1)

            pool.wait_ge(numbers_set, 4)
            pool.wait_ge(consts_loaded, 16)
            with pool.Fori(0, DEPTH) as l:
                norm_factors(l * PHASES)
                pool.wait_ge(bias_loaded, l * 16 + 16)
                rows = bias[:, :, :, :].rearrange("p h r k -> p (h r) k")
                pool.tensor_tensor(rows, rows, na_mask.unsqueeze(1).to_broadcast([P, NA_HEADS * BIAS_ROWS, GRID_W]),
                                   ALU.add).then_inc(bias_ready, 1)
                norm_factors(l * PHASES + 1)
                for i in range(GROUPS):
                    rope(l, i)
                pool.wait_ge(mix_ready, l + 1)
                pool.wait_ge(o_read, l * PAIRS + DIL_PAIRS)
                oh = o_dil[:, :, :, :].rearrange("p h t d -> p (h t) d")
                wts = mix_d[:, :, :].rearrange("p g j -> p (g j)").unsqueeze(2).to_broadcast([P, DIL_HEADS * TT, HD])
                pool.tensor_tensor(oh, oh, wts, ALU.mult).then_inc(mix_part, 1)
                pool.wait_ge(mix_part, l * 2 + 1)
                og = [o_dil[:, g * GROUP_HEADS:(g + 1) * GROUP_HEADS, :, :] for g in range(GROUPS)]
                pool.tensor_tensor(og[0], og[0], og[1], ALU.add).then_inc(mix_part, 1)
                pool.wait_ge(mix_part, l * 2 + 2)
                ya = y[:, :, 0:GROUP_HEADS * HD].rearrange("p t (h d) -> p h t d", h=GROUP_HEADS)
                pool.tensor_tensor(ya, og[0], og[2], ALU.add).then_inc(y_dil_done, 1)
                norm_factors(l * PHASES + 2)
            norm_factors(DEPTH * PHASES)

        @block.scalar
        def _(act):
            act.dma_start(x[:, :, :], x_in.rearrange("(t p) n -> p t n", p=P)).then_inc(x_loaded, 16)
            act.dma_start(cst[:, :], consts).then_inc(consts_loaded, 16)

            def hi(l, at, u, c=None):
                slot = (at + u) % RING
                n = l * L_UNITS + at + u
                turn = l * (L_UNITS // RING) + (at + u) // RING + 1
                if c is not None:
                    n = n + c * 3
                    turn = turn + c
                act.wait_ge(raw_arrived[slot], turn * 32)
                act.wait_ge(split_free, n + 1)
                act.activation(w_hi[slot][:, :], raw[slot][:, :], ACT.Copy).then_inc(hi_done, 1)

            def transposed_hi(ph):
                for g, (t, n) in enumerate(GROUP4):
                    act.wait_ge(xT_done, ph * 4 + g + 1)
                    act.activation(a_hi[:, 4 * n:4 * n + 4, t * P:(t + 1) * P],
                                   bank[TR[g % 2]][:, :].rearrange("p (k s) -> p k s", k=4), ACT.Copy).then_inc(xT_hi, 1)

            def sum_squares(ph):
                for t in range(TT):
                    act.activation(squares, x[:, t, :], ACT.Square, accum_out=sum_sq[:, t:t + 1]).then_inc(squares_done, 1)
                    if t == 0:
                        act.wait_ge(squares_done, ph * TT + 1)

            def feed_forward(l, f, at, prefetch):
                ph = l * PHASES + 2 * f
                ff = l * 2 + f
                transposed_hi(ph)
                act.wait_ge(xg_ready, ph * 4 + 4)
                sum_squares(ph)
                hi(l, at, 2)

                def tanh(c):
                    for t in range(TT):
                        if t == 0:
                            act.wait_ge(up_done, ff * CHUNKS + c + 1)
                        else:
                            unit_used(act, l, at, *((1, None) if isinstance(c, int) and c == 0 else (0, c)))
                        act.activation(tanh_g[:, t, :], bank[UP[t]][:, 0:FC], ACT.Tanh,
                                       scale=half_rstd[:, t:t + 1]).then_inc(tanh_done, 1)

                def hT_upper(c):
                    act.wait_ge(hT_done, ff * CHUNKS + c + 1)
                    act.activation(hT_hi[:, :, :], bank[HT][:, :].rearrange("p (k s) -> p k s", k=2),
                                   ACT.Copy).then_inc(hT_hi_done, 1)

                act.wait_ge(rstd_ready, ph + 1)
                tanh(0)
                with act.Fori(1, CHUNKS) as c:
                    hi(l, at, 0, c)
                    hi(l, at, 1, c)
                    hT_upper(c - 1)
                    hi(l, at, 2, c)
                    tanh(c)
                if prefetch:
                    hi(l, at, F_UNITS)
                hT_upper(CHUNKS - 1)
                if prefetch:
                    hi(l, at, F_UNITS + 1)

            def mixer(l):
                ph = l * PHASES + 1
                transposed_hi(ph)
                act.wait_ge(xg_ready, ph * 4 + 4)
                sum_squares(ph)
                for m in range(M_UNITS):
                    hi(l, M_AT, m + 2)
                    if m == 1:
                        act.wait_ge(rstd_ready, ph + 1)
                    for j, i in enumerate(QK_CHUNKS):
                        if m == chunk_steps(i)[-1] + 2:
                            act.wait_ge(qkT_done, l * 5 + j + 1)
                            for s in range(2):
                                ft = bank[PROJ[i % 2][s]][:, :].rearrange("p (f s) -> p f s", f=2)
                                if i < GROUPS:
                                    dst = (qT, kT)[s][:, 2 * i:2 * i + 2, :]
                                else:
                                    at = DIL_PAIRS + 2 * s
                                    dst = (qT, kT)[i - 5][:, at:at + 2, :]
                                is_q = (i < GROUPS and s == 0) or i == 5
                                act.activation(dst, ft, ACT.Copy, scale=HD ** -0.5 if is_q else 1.0).then_inc(qkT_read, 1)
                    i, _ = step_chunk(m - 1)
                    if i is not None and chunk_steps(i)[-1] == m - 1:
                        if 1 <= i < GROUPS or i == 5:
                            act.wait_ge(rope_dve, l * GROUPS + min(i, GROUPS))
                            act.wait_ge(rope_pool, l * GROUPS + min(i, GROUPS))
                        if i == 6:
                            act.wait_ge(qkT_done, l * 5 + 4)
                        for t in range(TT):
                            if t == 0:
                                act.wait_ge(proj_done, l * PROJ_CHUNKS + i + 1)
                            else:
                                unit_used(act, l, M_AT, m - 1)
                            src = bank[PROJ[i % 2][t]]
                            if i >= 8:
                                g0 = (i - 8) * NB
                                act.activation(gates[:, t, g0:g0 + NB], src[:, :], ACT.Tanh,
                                               scale=half_rstd[:, t:t + 1]).then_inc(gates_done, 1)
                                continue
                            w = NB
                            if i in (3, 4, 7):
                                v0 = {3: 0, 4: NB, 7: DIL_W}[i]
                                w = DIL_W - NB if i == 4 else NB
                                dst = v[:, t, v0:v0 + w]
                            else:
                                dst = qk_raw[:, t, :]
                            act.activation(dst, src[:, 0:w], ACT.Copy, scale=rstd[:, t:t + 1]).then_inc(proj_read, 1)
                    p = step_pair(m)
                    if p is not None:
                        for hh in range(2):
                            h = 2 * p + hh
                            act.wait_ge(neg_top_done, l * HEADS + h + 1)
                            for t in range(TT):
                                e = act.activation(probs[:, hh, t, :], probs[:, hh, t, :], ACT.Exp,
                                                   bias=neg_top[:, h, t:t + 1], accum_out=den[:, h, t:t + 1])
                            e.then_inc(exp_done, 1)
                    if m == pair_step(DIL_PAIRS - 1) + 1:
                        act.wait_ge(mix_exp_in, l + 1)
                        act.activation(mix_e[:, :, :], mix_d[:, :, :], ACT.Exp).then_inc(mix_exp, 1)
                    if m == Y_AT:
                        for j in range(3):
                            act.wait_ge(yT_done, l * 3 + j + 1)
                            act.activation(yT_hi[:, 2 * j:2 * j + 2, :], bank[YT[j]][:, :].rearrange("p (f s) -> p f s", f=2),
                                           ACT.Copy).then_inc(yT_hi_done, 1)
                    if m == O_AT - 1:
                        for g, (t, n) in enumerate(HALF_MAJOR):
                            act.wait_ge(mT_done, l * 4 + g + 1)
                            act.activation(a_hi[:, 4 * n:4 * n + 4, t * P:(t + 1) * P],
                                           bank[MT[g % 2]][:, :].rearrange("p (k s) -> p k s", k=4),
                                           ACT.Copy).then_inc(mT_hi, 1)

            act.wait_ge(x_loaded, 16)
            with act.Fori(0, DEPTH) as l:
                hi(l, F1_AT, 0)
                hi(l, F1_AT, 1)
                feed_forward(l, 0, F1_AT, True)
                mixer(l)
                feed_forward(l, 1, F2_AT, False)
            act.wait_ge(x_updated, DEPTH * 12)
            sum_squares(DEPTH * PHASES)

        @block.vector
        def _(dve):
            for i in range(2 * RING):
                dve.memset(credits[:, i:i + 1], 0.0).then_inc((lo_done, split_free)[i % 2], 1)

            def lo(l, at, u, c=None):
                slot = (at + u) % RING
                n = l * L_UNITS + at + u
                if c is not None:
                    n = n + c * 3
                dve.wait_ge(hi_done, n + 1)
                dve.tensor_tensor(w_lo[slot][:, :], raw[slot][:, :], w_hi[slot][:, :].bitcast(F32),
                                  ALU.subtract).then_inc(lo_done, 1)

            def update(l, ph, end, g):
                t, n = GROUP4[g]
                k = (ph - 1) * 4 + g + 1
                if g < 3:
                    dve.wait_ge(acc_done, (ph - 1) * 3 + g + 1)
                else:
                    unit_used(dve, l, end, -1)
                part = x[:, t, n * NB:(n + 1) * NB]
                dve.scalar_tensor_tensor(part, bank[ACC[t][n]][:, :], 0.5, part, ALU.mult, ALU.add).then_inc(x_updated, 1)
                return k

            def scaled(ph, g, updated=None):
                t, n = GROUP4[g]
                if updated is not None:
                    dve.wait_ge(x_updated, updated)
                dve.tensor_tensor(xg[:, t, n * NB:(n + 1) * NB], x[:, t, n * NB:(n + 1) * NB],
                                  gain[:, n * NB:(n + 1) * NB], ALU.mult).then_inc(xg_ready, 1)

            def transposed_lo(ph, g):
                t, n = GROUP4[g]
                dve.wait_ge(xT_hi, ph * 4 + g + 1)
                dve.tensor_tensor(a_lo[:, 4 * n:4 * n + 4, t * P:(t + 1) * P],
                                  bank[TR[g % 2]][:, :].rearrange("p (k s) -> p k s", k=4),
                                  a_hi[:, 4 * n:4 * n + 4, t * P:(t + 1) * P].bitcast(F32),
                                  ALU.subtract).then_inc(xT_lo, 1)

            def phase_input(l, ph, at, with_update):
                dve.wait_ge(gain_loaded, ph * 16 + 16)
                for g in range(4):
                    k = update(l, ph, at, g) if with_update else None
                    scaled(ph, g, k)
                    if g >= 1:
                        transposed_lo(ph, g - 1)
                transposed_lo(ph, 3)

            def feed_forward(l, f, at, prefetch, with_update):
                ph = l * PHASES + 2 * f
                ff = l * 2 + f
                phase_input(l, ph, at, with_update)
                lo(l, at, 2)
                dve.wait_ge(rstd_ready, ph + 1)

                def hide(c):
                    for t in range(TT):
                        k = ff * 2 * CHUNKS + c * 2 + t + 1
                        dve.wait_ge(tanh_done, k)
                        dve.scalar_tensor_tensor(gated[:, t, :], tanh_g[:, t, :], 1.0, bank[UP[t]][:, 0:FC],
                                                 ALU.add, ALU.mult).then_inc(gated_done, 1)
                        dve.wait_ge(gated_done, k)
                        dve.scalar_tensor_tensor(hidden[:, t, :], gated[:, t, :], half_rstd2[:, t:t + 1],
                                                 bank[UP[t]][:, FC:2 * FC], ALU.mult, ALU.mult).then_inc(hidden_done, 1)

                def hT_lower(c):
                    dve.wait_ge(hT_hi_done, ff * CHUNKS + c + 1)
                    dve.tensor_tensor(hT_lo[:, :, :], bank[HT][:, :].rearrange("p (k s) -> p k s", k=2),
                                      hT_hi[:, :, :].bitcast(F32), ALU.subtract).then_inc(hT_lo_done, 1)

                hide(0)
                with dve.Fori(1, CHUNKS) as c:
                    lo(l, at, 0, c)
                    lo(l, at, 1, c)
                    hT_lower(c - 1)
                    lo(l, at, 2, c)
                    hide(c)
                if prefetch:
                    lo(l, at, F_UNITS)
                hT_lower(CHUNKS - 1)
                if prefetch:
                    lo(l, at, F_UNITS + 1)

            def rope(l, i):
                heads = qk_raw[:, :, :].rearrange("p t (h s d) -> p t h s d", h=8, s=2)
                turned = qk_rot.rearrange("p t (h s d) -> p t h s d", h=8, s=2)
                c = cos.unsqueeze(2).to_broadcast([P, TT, 8, HALF])
                s = sin.unsqueeze(2).to_broadcast([P, TT, 8, HALF])
                dve.wait_ge(proj_read, l * 16 + 2 * i + 2)
                if i >= 1:
                    dve.wait_ge(qkT_done, l * 5 + i)
                dve.tensor_tensor(rope_tmp[:, 0], heads[:, :, :, 0, :], c, ALU.mult).then_inc(rope_dve_part, 1)
                dve.tensor_tensor(rope_tmp[:, 1], heads[:, :, :, 1, :], s, ALU.mult).then_inc(rope_dve_part, 1)
                dve.wait_ge(rope_dve_part, l * 6 + 2 * i + 2)
                dve.tensor_tensor(turned[:, :, :, 0, :], rope_tmp[:, 0], rope_tmp[:, 1], ALU.subtract).then_inc(rope_dve, 1)

            def probs_turned(l, h):
                dve.wait_ge(probsT_done, l * HEADS + h + 1)
                if h >= 2:
                    dve.wait_ge(pv_done, l * HEADS + h - 1)
                dve.tensor_copy(probsT[:, h % 2, :, :], bank[PT][:, :].rearrange("p (k q) -> p k q", k=TT)).then_inc(probsT_read, 1)

            def masked(l, h):
                hh = h % 2
                dve.wait_ge(scores_done, l * HEADS + h + 1)
                if h >= 2:
                    dve.wait_ge(probsT_done, l * HEADS + h - 1)
                dve.memset(wait_carrier[:, :], 0.0)
                for t in range(TT):
                    sc = bank[SC[hh]][:, t * SEQ:(t + 1) * SEQ]
                    to = probs[:, hh, t, :]
                    if h < DIL_HEADS:
                        more = dil_mask[:, h // GROUP_HEADS, t, :]
                    else:
                        sc = sc.rearrange("p (r k) -> p r k", k=GRID_W)
                        to = to.rearrange("p (r k) -> p r k", k=GRID_W)
                        more = bias[:, h - DIL_HEADS, 2 - 2 * t:6 - 2 * t, :]
                    r = dve.tensor_tensor_reduce(to, sc, more, 1.0, -3.0e38, ALU.add, ALU.max, top[:, h, t:t + 1])
                r.then_inc(scores_read, 1)
                dve.wait_ge(scores_read, l * HEADS + h + 1)
                dve.tensor_scalar(neg_top[:, h, :], top[:, h, :], -1.0, None, ALU.mult).then_inc(neg_top_done, 1)

            def products_read(l, p):
                src = bank[OB][:, 0:2 * TT * HD].rearrange("p (h t d) -> p h t d", h=2, t=TT)
                if p < DIL_PAIRS:
                    dve.wait_ge(pv_done, l * HEADS + 2 * p + 2)
                    dve.tensor_copy(o_dil[:, 2 * p:2 * p + 2, :, :], src).then_inc(o_read, 1)
                    return
                j = p - DIL_PAIRS
                dve.reciprocal(rden[:, :, :], den[:, 2 * p:2 * p + 2, :]).then_inc(rden_done, 1)
                dve.wait_ge(rden_done, l * (PAIRS - DIL_PAIRS) + j + 1)
                dve.wait_ge(pv_done, l * HEADS + 2 * p + 2)
                at = GROUP_HEADS * HD + 2 * j * HD
                dst = y[:, :, at:at + 2 * HD].rearrange("p t (h d) -> p h t d", h=2)
                dve.tensor_tensor(dst, src, rden[:, :, :].unsqueeze(3).to_broadcast([P, 2, TT, HD]),
                                  ALU.mult).then_inc(o_read, 1)

            def mix_weights(l):
                n = [0]
                tops = top[:, 0:DIL_HEADS, :].rearrange("p (g h) t -> p g (h t)", g=GROUPS)
                dens = den[:, 0:DIL_HEADS, :].rearrange("p (g h) t -> p g (h t)", g=GROUPS)

                def chained(ins):
                    ins.then_inc(mix_chain, 1)
                    n[0] += 1
                    dve.wait_ge(mix_chain, l * 6 + n[0])
                peak = mix[:, 1, :]
                chained(dve.tensor_tensor(mix[:, 0, :], tops[:, 0, :], tops[:, 1, :], ALU.max))
                chained(dve.tensor_tensor(peak, mix[:, 0, :], tops[:, 2, :], ALU.max))
                dve.tensor_tensor(mix_d[:, :, :], tops, peak.unsqueeze(1).to_broadcast([P, GROUPS, GROUP_HEADS * TT]),
                                  ALU.subtract).then_inc(mix_exp_in, 1)
                dve.wait_ge(mix_exp, l + 1)
                chained(dve.tensor_tensor(mix_d[:, :, :], mix_e[:, :, :], dens, ALU.mult))
                chained(dve.tensor_tensor(mix[:, 2, :], mix_d[:, 0, :], mix_d[:, 1, :], ALU.add))
                chained(dve.tensor_tensor(mix[:, 3, :], mix[:, 2, :], mix_d[:, 2, :], ALU.add))
                chained(dve.reciprocal(mix[:, 4, :], mix[:, 3, :]))
                dve.tensor_tensor(mix_d[:, :, :], mix_e[:, :, :],
                                  mix[:, 4, :].unsqueeze(1).to_broadcast([P, GROUPS, GROUP_HEADS * TT]),
                                  ALU.mult).then_inc(mix_ready, 1)

            def mixer(l):
                ph = l * PHASES + 1
                phase_input(l, ph, M_AT, True)
                for m in range(M_UNITS):
                    p = step_pair(m)
                    before = step_pair(m - 1)
                    for hh in range(2):
                        if before is not None:
                            probs_turned(l, 2 * before + hh)
                        if p is not None:
                            if p == DIL_PAIRS and hh == 0:
                                dve.wait_ge(bias_ready, l + 1)
                            masked(l, 2 * p + hh)
                    lo(l, M_AT, m + 2)
                    if m in (2, 4, 6):
                        rope(l, m // 2 - 1)
                    if before is not None:
                        products_read(l, before)
                    if before == DIL_PAIRS - 1:
                        mix_weights(l)
                    if m == Y_AT:
                        for j in range(3):
                            dve.wait_ge(yT_hi_done, l * 3 + j + 1)
                            dve.tensor_tensor(yT_lo[:, 2 * j:2 * j + 2, :],
                                              bank[YT[j]][:, :].rearrange("p (f s) -> p f s", f=2),
                                              yT_hi[:, 2 * j:2 * j + 2, :].bitcast(F32), ALU.subtract).then_inc(yT_lo_done, 1)
                    if m == BA_AT:
                        dve.wait_ge(gates_done, l * 8 + 8)
                        for g, (t, n) in enumerate(GROUP4):
                            if g < 3:
                                dve.wait_ge(a_done, l * 3 + g + 1)
                            else:
                                unit_used(dve, l, M_AT, BA_AT)
                            dve.scalar_tensor_tensor(merged[:, t, n * NB:(n + 1) * NB], gates[:, t, n * NB:(n + 1) * NB], 1.0,
                                                     bank[BANK_A[t][n]][:, :], ALU.add, ALU.mult).then_inc(a_read, 1)
                    if m == O_AT - 1:
                        dve.wait_ge(a_read, l * 4 + 4)
                        for g, (t, n) in enumerate(HALF_MAJOR):
                            if g < 3:
                                dve.wait_ge(b_done, l * 3 + g + 1)
                            else:
                                unit_used(dve, l, M_AT, O_AT - 1)
                            if g >= 1:
                                dve.wait_ge(merged_done, l * 4 + g)
                            dve.scalar_tensor_tensor(from_b, gates[:, t, D + n * NB:D + (n + 1) * NB], 1.0,
                                                     bank[BANK_B[t][n]][:, :], ALU.add, ALU.mult).then_inc(b_read, 1)
                            dve.wait_ge(b_read, l * 4 + g + 1)
                            part = merged[:, t, n * NB:(n + 1) * NB]
                            dve.tensor_tensor(part, part, from_b, ALU.add).then_inc(merged_done, 1)
                            if g >= 1:
                                merged_lo(l, g - 1)
                        merged_lo(l, 3)

            def merged_lo(l, g):
                t, n = HALF_MAJOR[g]
                dve.wait_ge(mT_hi, l * 4 + g + 1)
                dve.tensor_tensor(a_lo[:, 4 * n:4 * n + 4, t * P:(t + 1) * P],
                                  bank[MT[g % 2]][:, :].rearrange("p (k s) -> p k s", k=4),
                                  a_hi[:, 4 * n:4 * n + 4, t * P:(t + 1) * P].bitcast(F32),
                                  ALU.subtract).then_inc(mT_lo, 1)

            dve.wait_ge(x_loaded, 16)
            dve.wait_ge(consts_loaded, 16)
            with dve.Fori(0, DEPTH) as l:
                lo(l, F1_AT, 0)
                lo(l, F1_AT, 1)
                feed_forward(l, 0, F1_AT, True, False)
                mixer(l)
                feed_forward(l, 1, F2_AT, False, True)
                for g in range(4):
                    update(l, l * PHASES + 3, L_UNITS, g)
                dve.wait_ge(x_updated, l * 12 + 12)
            dve.wait_ge(gain_loaded, (DEPTH * PHASES + 1) * 16)
            dve.wait_ge(rstd_ready, DEPTH * PHASES + 1)
            for t in range(TT):
                dve.scalar_tensor_tensor(xg[:, t, :], x[:, t, :], rstd[:, t:t + 1], gain[:, :],
                                         ALU.mult, ALU.mult).then_inc(result_ready, 1)

        @block.tensor
        def _(pe):
            def product(dst, s_hi, s_lo, m_hi, m_lo, start, stop):
                pe.matmul(dst, s_hi, m_hi, start=start, stop=False)
                pe.matmul(dst, s_hi, m_lo, start=False, stop=False)
                return pe.matmul(dst, s_lo, m_hi, start=False, stop=stop)

            def split_ready(l, at, u, c=None):
                n = l * L_UNITS + at + u
                if c is not None:
                    n = n + c * 3
                pe.wait_ge(lo_done, n + 1 + RING)

            def cols(slot, t, a, dst, start, stop, js=range(4), nk=4):
                w = UNIT // nk
                for j in js:
                    k = nk * a + j
                    mm = product(dst[:, 0:w], a_hi[:, k, t * P:(t + 1) * P], a_lo[:, k, t * P:(t + 1) * P],
                                 w_hi[slot][:, j * w:(j + 1) * w], w_lo[slot][:, j * w:(j + 1) * w],
                                 start and j == 0, stop and j == nk - 1)
                return mm

            def rows(slot, s_hi, s_lo, k0, t, n, dst, start, stop):
                for j in range(2):
                    at = j * D + n * NB
                    mm = product(dst[:, :], s_hi[:, k0 + j, t * P:(t + 1) * P], s_lo[:, k0 + j, t * P:(t + 1) * P],
                                 w_hi[slot][:, at:at + NB], w_lo[slot][:, at:at + NB], start and j == 0, stop and j == 1)
                return mm

            def input_transposes(ph, gs):
                for g in gs:
                    t, n = GROUP4[g]
                    pe.wait_ge(xg_ready, ph * 4 + g + 1)
                    if g >= 2:
                        pe.wait_ge(xT_lo, ph * 4 + g - 1)
                    for j in range(4):
                        c = n * NB + j * P
                        tr = pe.transpose(bank[TR[g % 2]][:, j * P:(j + 1) * P], xg[:, t, c:c + P], ident)
                    tr.then_inc(xT_done, 1)

            def feed_forward(l, f, at):
                ph = l * PHASES + 2 * f
                ff = l * 2 + f

                def up(c, a, t, slot):
                    mm = cols(slot, t, a, bank[UP[t]], a == 0, a == 1)
                    if t == 1:
                        mm.then_inc(split_free, 1)
                    elif a == 1:
                        mm.then_inc(up_done, 1)

                def turn(c):
                    pe.wait_ge(hidden_done, ff * 2 * CHUNKS + c * 2 + 2)
                    for j in range(2):
                        for t in range(TT):
                            tr = pe.transpose(bank[HT][:, j * SEQ + t * P:j * SEQ + (t + 1) * P],
                                              hidden[:, t, j * P:(j + 1) * P], ident)
                    tr.then_inc(hT_done, 1)

                def down(c, slot, start, stop):
                    pe.wait_ge(hT_lo_done, ff * CHUNKS + c + 1)
                    for g, (t, n) in enumerate(GROUP4):
                        mm = rows(slot, hT_hi, hT_lo, 0, t, n, bank[ACC[t][n]], start, stop)
                        if g == 3:
                            mm.then_inc(split_free, 1)
                        elif stop:
                            mm.then_inc(acc_done, 1)

                input_transposes(ph, (0, 1))
                split_ready(l, at, 0)
                pe.wait_ge(xT_lo, ph * 4 + 1)
                up(0, 0, 0, 0)
                input_transposes(ph, (2, 3))
                pe.wait_ge(xT_lo, ph * 4 + 3)
                up(0, 0, 1, 0)
                split_ready(l, at, 1)
                up(0, 1, 0, 1)
                pe.wait_ge(xT_lo, ph * 4 + 4)
                up(0, 1, 1, 1)

                def chunk(c, first):
                    split_ready(l, at, -1, c)
                    for t in range(TT):
                        pe.wait_ge(hidden_done, ff * 2 * CHUNKS + (c - 1) * 2 + t + 1)
                        up(c, 0, t, 2)
                    turn(c - 1)
                    split_ready(l, at, 0, c)
                    for t in range(TT):
                        up(c, 1, t, 0)
                    split_ready(l, at, 1, c)
                    down(c - 1, 1, first, False)

                chunk(1, True)
                with pe.Fori(2, CHUNKS) as c:
                    chunk(c, False)
                turn(CHUNKS - 1)
                split_ready(l, at, F_UNITS - 1)
                down(CHUNKS - 1, 2, False, True)

            def qk_transposes(l, j, i):
                if i < GROUPS:
                    pe.wait_ge(rope_dve, l * GROUPS + i + 1)
                    pe.wait_ge(rope_pool, l * GROUPS + i + 1)
                    src = qk_rot
                else:
                    pe.wait_ge(proj_read, l * 16 + 2 * i + 2)
                    src = qk_raw
                for f in range(4):
                    for t in range(TT):
                        at = (f % 2) * SEQ + t * P
                        tr = pe.transpose(bank[PROJ[i % 2][f // 2]][:, at:at + P], src[:, t, f * P:(f + 1) * P], ident)
                tr.then_inc(qkT_done, 1)

            def scores(l, h):
                p, hh = h // 2, h % 2
                rows_ = slice(hh * HD, (hh + 1) * HD)
                for t in range(TT):
                    mm = pe.matmul(bank[SC[hh]][:, t * SEQ:(t + 1) * SEQ], qT[rows_, p, t * P:(t + 1) * P],
                                   kT[rows_, p, :], start=True, stop=True)
                mm.then_inc(scores_done, 1)

            def turn_probs(l, h):
                pe.wait_ge(exp_done, l * HEADS + h + 1)
                if h >= 1:
                    pe.wait_ge(probsT_read, l * HEADS + h)
                for k in range(TT):
                    for t in range(TT):
                        tr = pe.transpose(bank[PT][:, k * SEQ + t * P:k * SEQ + (t + 1) * P],
                                          probs[:, h % 2, t, k * P:(k + 1) * P], ident)
                tr.then_inc(probsT_done, 1)

            def times_v(l, h):
                p, hh = h // 2, h % 2
                pe.wait_ge(probsT_read, l * HEADS + h + 1)
                if hh == 0:
                    if p >= 1:
                        pe.wait_ge(o_read, l * PAIRS + p)
                    pe.wait_ge(proj_read, l * 16 + (10 if p < DIL_PAIRS else 16))
                for t in range(TT):
                    for k in range(TT):
                        at = (hh * TT + t) * HD
                        mm = pe.matmul(bank[OB][:, at:at + HD], probsT[:, hh, k, t * P:(t + 1) * P],
                                       v[:, k, h * HD:(h + 1) * HD], start=k == 0, stop=k == TT - 1)
                mm.then_inc(pv_done, 1)

            def mixer(l):
                ph = l * PHASES + 1
                input_transposes(ph, (0, 1))
                for m in range(O_AT):
                    slot = (M_AT + m) % RING
                    p, before = step_pair(m), step_pair(m - 1)
                    for j, i in enumerate(QK_CHUNKS):
                        if m == chunk_steps(i)[-1] + 2:
                            qk_transposes(l, j, i)
                    if before is not None:
                        turn_probs(l, 2 * before)
                    if p is not None:
                        pe.wait_ge(qkT_read, l * 10 + (2 * (p // 2) + 2 if p < DIL_PAIRS else 10))
                        if p >= 1:
                            pe.wait_ge(scores_read, l * HEADS + 2 * p)
                        scores(l, 2 * p)
                        scores(l, 2 * p + 1)
                    if m == Y_AT:
                        pe.wait_ge(y_dil_done, l + 1)
                        pe.wait_ge(o_read, l * PAIRS + PAIRS)
                        for j in range(3):
                            for f in range(2):
                                for t in range(TT):
                                    at = f * SEQ + t * P
                                    c = (2 * j + f) * P
                                    tr = pe.transpose(bank[YT[j]][:, at:at + P], y[:, t, c:c + P], ident)
                            tr.then_inc(yT_done, 1)
                    i, a = step_chunk(m)
                    if i is not None:
                        if a == 0 and i >= 2:
                            if i - 2 in QK_CHUNKS:
                                pe.wait_ge(qkT_read, l * 10 + 2 * QK_CHUNKS.index(i - 2) + 2)
                            elif i - 2 < 8:
                                pe.wait_ge(proj_read, l * 16 + 2 * (i - 2) + 2)
                            else:
                                pe.wait_ge(gates_done, l * 8 + 2 * (i - 10) + 2)
                        split_ready(l, M_AT, m)
                        last = a == len(chunk_steps(i)) - 1
                        nk = 8 if i == 4 else 4
                        for t in range(TT):
                            if m < 2:
                                if m == 0 and t == 1:
                                    input_transposes(ph, (2, 3))
                                pe.wait_ge(xT_lo, ph * 4 + 2 * t + m + 1)
                            for q in range(2):
                                js = range(q * nk // 2, (q + 1) * nk // 2)
                                mm = cols(slot, t, a, bank[PROJ[i % 2][t]], a == 0, last, js, nk)
                                if q == 1 and t == 1:
                                    mm.then_inc(split_free, 1)
                                elif q == 1 and last:
                                    mm.then_inc(proj_done, 1)
                                if before is not None:
                                    if t == 0 and q == 0:
                                        turn_probs(l, 2 * before + 1)
                                    if t == 0 and q == 1:
                                        times_v(l, 2 * before)
                                    if t == 1 and q == 0:
                                        times_v(l, 2 * before + 1)
                    elif m == BA_AT:
                        split_ready(l, M_AT, m)
                        pe.wait_ge(yT_lo_done, l * 3 + 3)
                        pe.wait_ge(gates_done, l * 8 + 6)
                        for g, (t, n) in enumerate(GROUP4):
                            mm = rows(slot, yT_hi, yT_lo, 0, t, n, bank[BANK_A[t][n]], True, True)
                            mm.then_inc(a_done if g < 3 else split_free, 1)
                    else:
                        split_ready(l, M_AT, m)
                        if m == BB_AT:
                            pe.wait_ge(gates_done, l * 8 + 8)
                        last = m == BB_AT + 1
                        for g, (t, n) in enumerate(HALF_MAJOR):
                            mm = rows(slot, yT_hi, yT_lo, 2 * (m - BB_AT) + 2, t, n, bank[BANK_B[t][n]], not last, last)
                            if g == 3:
                                mm.then_inc(split_free, 1)
                            elif last:
                                mm.then_inc(b_done, 1)

                def merged_transposes(gs):
                    for g in gs:
                        t, n = HALF_MAJOR[g]
                        pe.wait_ge(merged_done, l * 4 + g + 1)
                        if g >= 2:
                            pe.wait_ge(mT_lo, l * 4 + g - 1)
                        for j in range(4):
                            c = n * NB + j * P
                            tr = pe.transpose(bank[MT[g % 2]][:, j * P:(j + 1) * P], merged[:, t, c:c + P], ident)
                        tr.then_inc(mT_done, 1)

                merged_transposes((0, 1))
                for j in range(4):
                    m = O_AT + j
                    split_ready(l, M_AT, m)
                    if j == 2:
                        pe.wait_ge(mT_lo, l * 4 + 4)
                    for g, (t, n) in enumerate(GROUP4):
                        if j == 0 and n == 0:
                            pe.wait_ge(mT_lo, l * 4 + t + 1)
                        mm = rows((M_AT + m) % RING, a_hi, a_lo, 2 * j, t, n, bank[ACC[t][n]], j == 0, j == 3)
                        if g == 3:
                            mm.then_inc(split_free, 1)
                        elif j == 3:
                            mm.then_inc(acc_done, 1)
                    if j == 0:
                        merged_transposes((2, 3))

            pe.wait_ge(consts_loaded, 16)
            with pe.Fori(0, DEPTH) as l:
                feed_forward(l, 0, F1_AT)
                mixer(l)
                feed_forward(l, 1, F2_AT)


_INS = ["ffn1_w_up", "ffn1_w_down", "ffn2_w_up", "ffn2_w_down", "w_in", "na_rel_bias", "w_branch_a", "w_branch_b", "w_out"]


def _constants():
    pos = np.arange(SEQ)
    rel = pos[None, :] - pos[:, None]
    parts = []
    for window, dilation in DIL_PATTERNS:
        half = window // 2 // dilation
        ok = (rel % dilation == 0) & (np.abs(rel) <= half * dilation)
        mask = np.where(ok, 0.0, NEG_INF).astype(np.float32)
        parts += [mask[t * P:(t + 1) * P] for t in range(TT)]
    qc = np.arange(P) % GRID_W
    low = np.clip(qc - NA_COLS // 2, 0, GRID_W - NA_COLS)[:, None]
    kc = np.arange(GRID_W)[None, :]
    parts.append(np.where((kc >= low) & (kc < low + NA_COLS), 0.0, NEG_INF).astype(np.float32))
    freq = np.float32(10000.0) ** (-np.arange(HALF, dtype=np.float32) / np.float32(HALF))
    angle = pos.astype(np.float32)[:, None] * freq[None, :]
    for table in (np.cos(angle), np.sin(angle)):
        parts += [table[t * P:(t + 1) * P].astype(np.float32) for t in range(TT)]
    parts.append(np.eye(P, dtype=np.float32))
    return np.concatenate(parts, axis=1)


def kernel(**inputs):
    import concourse.bacc as _bacc
    from concourse.bass_utils import run_bass_kernel_spmd as _run

    nc = _bacc.Bacc("TRN2", target_bir_lowering=False, num_devices=1)
    rows = [inputs[name][l] for l in range(DEPTH) for name in ("ffn1_norm", "mix_norm", "ffn2_norm")]
    arrays = {name: np.ascontiguousarray(inputs[name]) for name in _INS}
    arrays["x"] = np.ascontiguousarray(inputs["x"]).reshape(SEQ, D)
    arrays["gains"] = np.stack(rows + [inputs["final_norm"]])
    arrays["consts"] = _constants()
    ap = {name: nc.dram_tensor(f"{name}_dram", a.shape, F32, kind="ExternalInput").ap() for name, a in arrays.items()}
    out = nc.dram_tensor("out_dram", (SEQ, D), F32, kind="ExternalOutput").ap()
    build(nc, ap["x"], ap["gains"], (ap["ffn1_w_up"], ap["ffn2_w_up"]), (ap["ffn1_w_down"], ap["ffn2_w_down"]),
          ap["w_in"], ap["na_rel_bias"], ap["w_branch_a"], ap["w_branch_b"], ap["w_out"], ap["consts"], out)
    r = _run(nc, [{f"{name}_dram": a for name, a in arrays.items()}], core_ids=[0])
    return r.results[0]["out_dram"].reshape(1, SEQ, D)
```

```python
from contextlib import ExitStack

import concourse.bass as bass
import numpy as np
from concourse import mybir

ALU = mybir.AluOpType
ACT = mybir.ActivationFunctionType
F32 = mybir.dt.float32
F32R = mybir.dt.float32r

P = 128
SEQ = 256
TT = SEQ // P
D = 1024
KT = D // P
DEPTH = 2
D_FF = 2816
HD = 64
HALF = HD // 2
DIL_PATTERNS = ((128, 1), (512, 4), (2048, 16))
GROUPS = len(DIL_PATTERNS)
GROUP_HEADS = 4
DIL_HEADS = GROUPS * GROUP_HEADS
NA_HEADS = 8
HEADS = DIL_HEADS + NA_HEADS
GRID_W = 64
NA_COLS = 16
REL_ROWS, REL_COLS = 15, 31
DIL_W = DIL_HEADS * HD
STRIDE = DIL_PATTERNS[1][1]
RUN = SEQ // STRIDE
assert all(d % STRIDE == 0 for _, d in DIL_PATTERNS[1:]) and P % RUN == 0
NA_W = NA_HEADS * HD
NA_AT = 3 * DIL_W
GATE_AT = NA_AT + 3 * NA_W
IN_WIDTH = GATE_AT + 2 * D
EPS = 1e-6
NEG_INF = -1e30

NB = 512
UNIT = 2048
RING = 3
FC = 256
CHUNKS = D_FF // FC
F_UNITS = 3 * CHUNKS
M_UNITS = 30
L_UNITS = 2 * F_UNITS + M_UNITS
F1_AT, M_AT, F2_AT = 0, F_UNITS, F_UNITS + M_UNITS
assert F_UNITS % RING == 0 and M_UNITS % RING == 0
PHASES = 3
PAIRS = HEADS // 2
DIL_PAIRS = DIL_HEADS // 2
BIAS_ROWS = 6

V_AT, VC_AT, NQ_AT, G_AT, BA_AT, BB_AT, O_AT = 6, 8, 9, 15, 23, 24, 26
PROJ_CHUNKS = 12
QK_CHUNKS = (0, 1, 2, 5, 6)
Y_AT = 22

C_MASK = 0
C_BLOCK = C_MASK + TT * SEQ
C_NAMASK = C_BLOCK + (GROUPS - 1) * P
C_COS = C_NAMASK + GRID_W
C_SIN = C_COS + TT * HALF
C_IDENT = C_SIN + TT * HALF
C_ALL = C_IDENT + P


def chunk_steps(i):
    if i < 4:
        return (2 * i, 2 * i + 1)
    if i == 4:
        return (VC_AT,)
    return (NQ_AT + 2 * (i - 5), NQ_AT + 2 * (i - 5) + 1)


def step_chunk(m):
    for i in range(PROJ_CHUNKS):
        if m in chunk_steps(i):
            return i, chunk_steps(i).index(m)
    return None, 0


def pair_step(p):
    return NQ_AT + p if p < DIL_PAIRS else G_AT + 1 + p - DIL_PAIRS


def step_pair(m):
    for p in range(PAIRS):
        if pair_step(p) == m:
            return p
    return None


def build(nc, x_in, gains, w_up, w_down, w_in, rel_bias, w_a, w_b, w_out, consts, out):
    bias_rows = nc.dram_tensor("bias_rows", [DEPTH, P, NA_HEADS, BIAS_ROWS, GRID_W], F32, kind="Internal").ap()
    with ExitStack() as ctx:
        def sb(name, shape, dt=F32):
            return ctx.enter_context(nc.sbuf_tensor(name, shape, dt))

        def sem(name):
            return ctx.enter_context(nc.semaphore(name))

        raw = [sb(f"raw{i}", [P, UNIT]) for i in range(RING)]
        w_hi = [sb(f"w_hi{i}", [P, UNIT], F32R) for i in range(RING)]
        w_lo = [sb(f"w_lo{i}", [P, UNIT], F32R) for i in range(RING)]
        x = sb("x", [P, TT, D])
        gain = sb("gain", [P, D])
        a_hi = sb("a_hi", [P, KT, SEQ], F32R)
        a_lo = sb("a_lo", [P, KT, SEQ], F32R)
        qT = sb("qT", [P, PAIRS, SEQ])
        kT = sb("kT", [P, PAIRS, SEQ])
        v = sb("v", [P, TT, HEADS * HD])
        qk_raw = sb("qk_raw", [P, TT, NB])
        gates = sb("gates", [P, TT, 2 * D])
        bias = sb("bias", [P, NA_HEADS, BIAS_ROWS, GRID_W])
        cst = sb("cst", [P, C_ALL])
        hT_hi = sb("hT_hi", [P, 2, SEQ], F32R)
        hT_lo = sb("hT_lo", [P, 2, SEQ], F32R)
        probs = sb("probs", [P, 2, TT, SEQ])
        probsT = sb("probsT", [P, 2, TT, SEQ])
        o_dil = sb("o_dil", [P, DIL_HEADS, TT, HD])
        y = sb("y", [P, TT, GROUP_HEADS * HD + NA_W])
        yT_hi = sb("yT_hi", [P, 6, SEQ], F32R)
        yT_lo = sb("yT_lo", [P, 6, SEQ], F32R)
        top = sb("top", [P, HEADS, TT])
        neg_top = sb("neg_top", [P, HEADS, TT])
        den = sb("den", [P, HEADS, TT])
        rden = sb("rden", [P, 2, TT])
        mix = sb("mix", [P, 6, GROUP_HEADS * TT])
        mix_e = sb("mix_e", [P, GROUPS, GROUP_HEADS * TT])
        mix_d = sb("mix_d", [P, GROUPS, GROUP_HEADS * TT])
        stat = sb("stat", [P, 8, TT])
        wait_carrier = sb("wait_carrier", [P, 1])
        credits = sb("credits", [P, 2 * RING])

        flat_gates = gates[:, :, :].rearrange("p t n -> p (t n)")
        xg = flat_gates[:, 0:TT * D].rearrange("p (t n) -> p t n", t=TT)
        rope_tmp = flat_gates[:, 0:4 * TT * 8 * HALF].rearrange("p (i t h d) -> p i t h d", i=4, t=TT, h=8)
        qk_rot = flat_gates[:, TT * D:TT * D + TT * NB].rearrange("p (t n) -> p t n", t=TT)
        flat_probs = probs[:, :, :, :].rearrange("p a t k -> p (a t k)")
        tanh_g = flat_probs[:, 0:TT * FC].rearrange("p (t n) -> p t n", t=TT)
        gated = flat_probs[:, TT * FC:2 * TT * FC].rearrange("p (t n) -> p t n", t=TT)
        hidden = probsT[:, :, :, :].rearrange("p a t k -> p (a t k)")[:, 0:TT * FC].rearrange("p (t n) -> p t n", t=TT)
        squares = flat_probs
        merged = qT[:, :, :].rearrange("p a b -> p (a b)")[:, 0:TT * D].rearrange("p (t n) -> p t n", t=TT)
        from_b = qk_raw[:, 0, :]

        near_mask = cst[:, C_MASK:C_BLOCK].rearrange("p (t k) -> p t k", t=TT)
        block_mask = cst[:, C_BLOCK:C_NAMASK].rearrange("p (g k) -> p g k", g=GROUPS - 1)
        na_mask = cst[:, C_NAMASK:C_COS]
        cos = cst[:, C_COS:C_SIN].rearrange("p (t d) -> p t d", t=TT)
        sin = cst[:, C_SIN:C_IDENT].rearrange("p (t d) -> p t d", t=TT)
        ident = cst[:, C_IDENT:C_ALL]
        sum_sq, rstd, half_rstd, half_rstd2 = (stat[:, i, :] for i in range(4))
        minus_half, half, one_over_d, eps = (stat[:, i, :] for i in range(4, 8))

        bank = [ctx.enter_context(nc.psum_tensor(f"bank{i}", [P, NB], F32)) for i in range(8)]
        UP = (0, 1)
        TR = (2, 3)
        HT = (2, 3)
        ACC = ((4, 5), (6, 7))
        PROJ = ((0, 1), (4, 5))
        SC = (6, 7)
        PT, OB = 2, 3
        YT = (6, 7, 2)
        BANK_A = ((0, 1), (6, 7))
        BANK_B = ((4, 2), (5, 3))
        MT = (0, 1)

        x_loaded = [sem(f"x_loaded{t}") for t in range(TT)]
        ident_loaded = sem("ident_loaded")
        consts_loaded = sem("consts_loaded")
        gain_loaded = sem("gain_loaded")
        bias_spread = sem("bias_spread")
        bias_loaded = sem("bias_loaded")
        bias_ready = sem("bias_ready")
        raw_arrived = [sem(f"raw_arrived{i}") for i in range(RING)]
        hi_done = sem("hi_done")
        lo_done = sem("lo_done")
        split_free = sem("split_free")
        x_updated = sem("x_updated")
        xg_ready = sem("xg_ready")
        xT_done = sem("xT_done")
        xT_hi = sem("xT_hi")
        xT_lo = sem("xT_lo")
        squares_done = sem("squares_done")
        pool_chain = sem("pool_chain")
        numbers_set = sem("numbers_set")
        rstd_ready = sem("rstd_ready")
        up_done = sem("up_done")
        tanh_done = sem("tanh_done")
        gated_done = sem("gated_done")
        hidden_done = sem("hidden_done")
        hT_done = sem("hT_done")
        hT_hi_done = sem("hT_hi_done")
        hT_lo_done = sem("hT_lo_done")
        acc_done = sem("acc_done")
        proj_done = sem("proj_done")
        proj_read = sem("proj_read")
        rope_dve = sem("rope_dve")
        rope_dve_part = sem("rope_dve_part")
        rope_pool = sem("rope_pool")
        rope_pool_part = sem("rope_pool_part")
        qkT_done = sem("qkT_done")
        qkT_read = sem("qkT_read")
        scores_done = sem("scores_done")
        scores_read = sem("scores_read")
        neg_top_done = sem("neg_top_done")
        exp_done = sem("exp_done")
        probsT_done = sem("probsT_done")
        probsT_read = sem("probsT_read")
        pv_done = sem("pv_done")
        rden_done = sem("rden_done")
        o_read = sem("o_read")
        mix_chain = sem("mix_chain")
        mix_exp_in = sem("mix_exp_in")
        mix_exp = sem("mix_exp")
        mix_ready = sem("mix_ready")
        mix_part = sem("mix_part")
        y_dil_done = sem("y_dil_done")
        gates_done = sem("gates_done")
        yT_done = sem("yT_done")
        yT_hi_done = sem("yT_hi_done")
        yT_lo_done = sem("yT_lo_done")
        a_done = sem("a_done")
        a_read = sem("a_read")
        b_done = sem("b_done")
        b_read = sem("b_read")
        merged_done = sem("merged_done")
        mT_done = sem("mT_done")
        mT_hi = sem("mT_hi")
        mT_lo = sem("mT_lo")
        result_ready = sem("result_ready")
        out_written = sem("out_written")

        GROUP4 = ((0, 0), (0, 1), (1, 0), (1, 1))
        HALF_MAJOR = ((0, 0), (1, 0), (0, 1), (1, 1))

        def residues(rows):
            return rows.rearrange("(j r) d -> r j d", r=STRIDE)

        def stream_part(tile, r):
            at = r * RUN % P
            return tile[at:at + RUN, r * RUN // P, :]

        def yT_parts(yT, j):
            dst = yT[:, 2 * j:2 * j + 2, :]
            src = bank[YT[j]][:, :].rearrange("p (f s) -> p f s", f=2)
            if j == 0:
                return dst, src
            return dst.rearrange("p f (r j) -> p f r j", r=STRIDE), src.rearrange("p f (j r) -> p f r j", r=STRIDE)

        def keys(h):
            return P if GROUP_HEADS <= h < DIL_HEADS else SEQ

        def unit_used(eng, l, at, u, c=None):
            n = l * L_UNITS + at + u + 1 + RING
            eng.wait_ge(split_free, n if c is None else n + c * 3)

        block = ctx.enter_context(nc.Block())

        @block.sync
        def _(sp):
            def unit(n, slot, parts):
                sp.wait_ge(lo_done, n + 1)
                for dst, src in parts(raw[slot]):
                    sp.dma_start(dst, src).then_inc(raw_arrived[slot], 16)

            def load_gain(row):
                sp.dma_start(gain[:, :], gains[row, :].partition_broadcast(P)).then_inc(gain_loaded, 16)

            def up_unit(f, l, c, a):
                src = w_up[f].rearrange("l (k p) n -> l p k n", p=P)

                def parts(place):
                    to = place[:, :].rearrange("p (k n) -> p k n", n=2 * FC)
                    for g in range(2):
                        cols = src[:, :, 4 * a:4 * a + 4, g * D_FF:(g + 1) * D_FF]
                        yield to[:, :, g * FC:(g + 1) * FC], cols[l, :, :, bass.ts(c, FC)]
                return parts

            def rows_unit(w, l, k0):
                src = w.rearrange("l (k p) n -> l p k n", p=P)

                def parts(place):
                    for j in range(2):
                        yield place[:, j * D:(j + 1) * D], src[l, :, k0 + j, :]
                return parts

            def down_unit(f, l, c):
                rows = w_down[f].rearrange("l (k p) n -> l k p n", p=P)

                def parts(place):
                    for j in range(2):
                        yield place[:, j * D:(j + 1) * D], rows[l, c * 2 + j, :, :]
                return parts

            def cols_unit(l, c0, a):
                src = w_in.rearrange("l (k p) n -> l p k n", p=P)

                def parts(place):
                    to = place[:, :].rearrange("p (k n) -> p k n", n=NB)
                    for j in range(2):
                        k = 4 * a + 2 * j
                        yield to[:, 2 * j:2 * j + 2, :], src[l, :, k:k + 2, c0:c0 + NB]
                return parts

            def qk_unit(l, g, a):
                src = w_in.rearrange("l (k p) n -> l p k n", p=P)
                w = GROUP_HEADS * HD

                def parts(place):
                    to = place[:, :].rearrange("p (k n) -> p k n", n=NB)
                    for j in range(2):
                        c0 = j * DIL_W + g * w
                        yield to[:, :, j * w:(j + 1) * w], src[l, :, 4 * a:4 * a + 4, c0:c0 + w]
                return parts

            def last_v_unit(l):
                src = w_in.rearrange("l (k p) n -> l p k n", p=P)
                c0 = 2 * DIL_W + NB

                def parts(place):
                    to = place[:, :].rearrange("p (k n) -> p k n", n=DIL_W - NB)
                    for j in range(2):
                        yield to[:, 4 * j:4 * j + 4, :], src[l, :, 4 * j:4 * j + 4, c0:NA_AT]
                return parts

            def feed_forward(f, l, at, next_gain):
                n0 = l * L_UNITS + at
                unit(n0, 0, up_unit(f, l, 0, 0))
                unit(n0 + 1, 1, up_unit(f, l, 0, 1))
                with sp.Fori(1, CHUNKS) as c:
                    unit(n0 + c * 3 - 1, 2, up_unit(f, l, c, 0))
                    unit(n0 + c * 3, 0, up_unit(f, l, c, 1))
                    unit(n0 + c * 3 + 1, 1, down_unit(f, l, c - 1))
                load_gain(next_gain)
                unit(n0 + F_UNITS - 1, 2, down_unit(f, l, CHUNKS - 1))

            sp.dma_start(gain[:, :], gains[0, :].partition_broadcast(P)).then_inc(gain_loaded, 16)
            with sp.Fori(0, DEPTH) as l:
                feed_forward(0, l, F1_AT, l * PHASES + 1)
                sp.wait_ge(bias_spread, 16 * DEPTH * 2 * BIAS_ROWS)
                sp.dma_start(bias[:, :, :, :].rearrange("p h r k -> p (h r k)"),
                             bias_rows.rearrange("l p h r k -> l p (h r k)")[l, :, :]).then_inc(bias_loaded, 16)
                n0 = l * L_UNITS + M_AT
                m = 0
                for g in range(GROUPS):
                    for a in range(2):
                        unit(n0 + m, m % RING, qk_unit(l, g, a))
                        m += 1
                for a in range(2):
                    unit(n0 + m, m % RING, cols_unit(l, 2 * DIL_W, a))
                    m += 1
                unit(n0 + m, m % RING, last_v_unit(l))
                m += 1
                for i in range(7):
                    for a in range(2):
                        unit(n0 + m, m % RING, cols_unit(l, NA_AT + i * NB, a))
                        m += 1
                unit(n0 + m, m % RING, rows_unit(w_a, l, 0))
                m += 1
                load_gain(l * PHASES + 2)
                for k0 in (0, 2):
                    unit(n0 + m, m % RING, rows_unit(w_b, l, k0))
                    m += 1
                for k0 in range(0, KT, 2):
                    unit(n0 + m, m % RING, rows_unit(w_out, l, k0))
                    m += 1
                feed_forward(1, l, F2_AT, l * PHASES + 3)
            for r in range(STRIDE):
                sp.wait_ge(result_ready, r * RUN // P + 1)
                sp.dma_start(residues(out)[r, :, :], stream_part(xg, r)).then_inc(out_written, 16)
            sp.wait_ge(out_written, 16 * STRIDE)

        @block.gpsimd
        def _(pool):
            for tile, number in ((minus_half, -0.5), (half, 0.5), (one_over_d, 1.0 / D), (eps, EPS)):
                pool.memset(tile, number).then_inc(numbers_set, 1)
            def norm_factors(ph):
                pool.wait_ge(squares_done, ph * TT + TT)
                pool.tensor_tensor(rstd, sum_sq, one_over_d, ALU.mult).then_inc(pool_chain, 1)
                pool.wait_ge(pool_chain, ph * 4 + 1)
                pool.tensor_tensor(rstd, rstd, eps, ALU.add).then_inc(pool_chain, 1)
                pool.wait_ge(pool_chain, ph * 4 + 2)
                pool.tensor_tensor(rstd, rstd, minus_half, ALU.pow).then_inc(pool_chain, 1)
                pool.wait_ge(pool_chain, ph * 4 + 3)
                pool.tensor_tensor(half_rstd, rstd, half, ALU.mult).then_inc(pool_chain, 1)
                pool.wait_ge(pool_chain, ph * 4 + 4)
                pool.tensor_tensor(half_rstd2, rstd, half_rstd, ALU.mult).then_inc(rstd_ready, 1)

            def rope(l, i):
                heads = qk_raw[:, :, :].rearrange("p t (h s d) -> p t h s d", h=8, s=2)
                turned = qk_rot.rearrange("p t (h s d) -> p t h s d", h=8, s=2)
                c = cos.unsqueeze(2).to_broadcast([P, TT, 8, HALF])
                s = sin.unsqueeze(2).to_broadcast([P, TT, 8, HALF])
                pool.wait_ge(proj_read, l * 16 + 2 * i + 2)
                if i >= 1:
                    pool.wait_ge(qkT_done, l * 5 + i)
                pool.tensor_tensor(rope_tmp[:, 2], heads[:, :, :, 1, :], c, ALU.mult).then_inc(rope_pool_part, 1)
                pool.tensor_tensor(rope_tmp[:, 3], heads[:, :, :, 0, :], s, ALU.mult).then_inc(rope_pool_part, 1)
                pool.wait_ge(rope_pool_part, l * 6 + 2 * i + 2)
                pool.tensor_tensor(turned[:, :, :, 1, :], rope_tmp[:, 2], rope_tmp[:, 3], ALU.add).then_inc(rope_pool, 1)

            pool.wait_ge(numbers_set, 4)
            norm_factors(0)
            for l in range(DEPTH):
                for a in range(2):
                    for r in range(BIAS_ROWS):
                        at = l * NA_HEADS * REL_ROWS * REL_COLS + (r - 2 - a + 7) * REL_COLS + NA_COLS - 1
                        src = bass.AP(rel_bias.tensor, at, [[REL_ROWS * REL_COLS, NA_HEADS], [-1, GRID_W], [1, GRID_W]])
                        dst = bias_rows[l, GRID_W * a:GRID_W * (a + 1), :, r, :].rearrange("q h k -> h q k")
                        pool.dma_start(dst, src).then_inc(bias_spread, 16)
            pool.wait_ge(consts_loaded, 16)
            with pool.Fori(0, DEPTH) as l:
                pool.wait_ge(bias_loaded, l * 16 + 16)
                rows = bias[:, :, :, :].rearrange("p h r k -> p (h r) k")
                pool.tensor_tensor(rows, rows, na_mask.unsqueeze(1).to_broadcast([P, NA_HEADS * BIAS_ROWS, GRID_W]),
                                   ALU.add).then_inc(bias_ready, 1)
                norm_factors(l * PHASES + 1)
                for i in range(GROUPS):
                    rope(l, i)
                pool.wait_ge(mix_ready, l + 1)
                pool.wait_ge(o_read, l * PAIRS + DIL_PAIRS)
                oh = o_dil[:, :, :, :].rearrange("p h t d -> p (h t) d")
                wts = mix_d[:, :, :].rearrange("p g j -> p (g j)").unsqueeze(2).to_broadcast([P, DIL_HEADS * TT, HD])
                pool.tensor_tensor(oh, oh, wts, ALU.mult).then_inc(mix_part, 1)
                pool.wait_ge(mix_part, l * 2 + 1)
                og = [o_dil[:, g * GROUP_HEADS:(g + 1) * GROUP_HEADS, :, :] for g in range(GROUPS)]
                pool.tensor_tensor(og[0], og[0], og[1], ALU.add).then_inc(mix_part, 1)
                pool.wait_ge(mix_part, l * 2 + 2)
                ya = y[:, :, 0:GROUP_HEADS * HD].rearrange("p t (h d) -> p h t d", h=GROUP_HEADS)
                pool.tensor_tensor(ya, og[0], og[2], ALU.add).then_inc(y_dil_done, 1)
                norm_factors(l * PHASES + 2)
                norm_factors(l * PHASES + 3)

        @block.scalar
        def _(act):
            def load_x(t):
                for r in range(t * P // RUN, (t + 1) * P // RUN):
                    act.dma_start(stream_part(x, r), residues(x_in)[r, :, :]).then_inc(x_loaded[t], 16)

            load_x(0)
            act.dma_start(ident, consts[:, C_IDENT:C_ALL]).then_inc(ident_loaded, 16)
            load_x(1)

            def hi(l, at, u, c=None):
                slot = (at + u) % RING
                n = l * L_UNITS + at + u
                turn = l * (L_UNITS // RING) + (at + u) // RING + 1
                if c is not None:
                    n = n + c * 3
                    turn = turn + c
                act.wait_ge(raw_arrived[slot], turn * 32)
                act.wait_ge(split_free, n + 1)
                act.activation(w_hi[slot][:, :], raw[slot][:, :], ACT.Copy).then_inc(hi_done, 1)

            def transposed_hi(ph, g):
                t, n = GROUP4[g]
                act.wait_ge(xT_done, ph * 4 + g + 1)
                act.activation(a_hi[:, 4 * n:4 * n + 4, t * P:(t + 1) * P],
                               bank[TR[g % 2]][:, :].rearrange("p (k s) -> p k s", k=4), ACT.Copy).then_inc(xT_hi, 1)

            def sum_squares(ph, t):
                act.wait_ge(xg_ready, ph * 4 + 2 * t + 2)
                if t == 1:
                    act.wait_ge(squares_done, ph * TT + 1)
                act.activation(squares, x[:, t, :], ACT.Square, accum_out=sum_sq[:, t:t + 1]).then_inc(squares_done, 1)

            def phase_input(l, ph, at):
                transposed_hi(ph, 0)
                transposed_hi(ph, 1)
                sum_squares(ph, 0)
                transposed_hi(ph, 2)
                sum_squares(ph, 1)
                hi(l, at, 2)
                transposed_hi(ph, 3)

            def next_hi(l, f, at, u):
                if f == 0:
                    hi(l, at, F_UNITS + u)
                else:
                    with act.If(DEPTH - 1 - l):
                        hi(l, at, F_UNITS + u)

            def feed_forward(l, f, at):
                ph = l * PHASES + 2 * f
                ff = l * 2 + f
                phase_input(l, ph, at)

                def tanh(c):
                    for t in range(TT):
                        if t == 0:
                            act.wait_ge(up_done, ff * CHUNKS + c + 1)
                        else:
                            unit_used(act, l, at, *((1, None) if isinstance(c, int) and c == 0 else (0, c)))
                        act.activation(tanh_g[:, t, :], bank[UP[t]][:, 0:FC], ACT.Tanh,
                                       scale=half_rstd[:, t:t + 1]).then_inc(tanh_done, 1)

                def hT_upper(c):
                    for t in range(TT):
                        toks = slice(t * P, (t + 1) * P)
                        act.wait_ge(hT_done, ff * 2 * CHUNKS + c * 2 + t + 1)
                        act.activation(hT_hi[:, :, toks], bank[HT[t]][:, 0:2 * P].rearrange("p (k s) -> p k s", k=2),
                                       ACT.Copy).then_inc(hT_hi_done, 1)

                act.wait_ge(rstd_ready, ph + 1)
                tanh(0)
                with act.Fori(1, CHUNKS) as c:
                    hi(l, at, 0, c)
                    hi(l, at, 1, c)
                    hT_upper(c - 1)
                    hi(l, at, 2, c)
                    tanh(c)
                next_hi(l, f, at, 0)
                hT_upper(CHUNKS - 1)
                next_hi(l, f, at, 1)

            def mixer(l):
                ph = l * PHASES + 1
                phase_input(l, ph, M_AT)
                for m in range(M_UNITS):
                    if m > 0:
                        hi(l, M_AT, m + 2)
                    if m == 1:
                        act.wait_ge(rstd_ready, ph + 1)
                    i, _ = step_chunk(m - 1)
                    if i is not None and chunk_steps(i)[-1] == m - 1:
                        if 1 <= i < GROUPS or i == 5:
                            act.wait_ge(rope_dve, l * GROUPS + min(i, GROUPS))
                            act.wait_ge(rope_pool, l * GROUPS + min(i, GROUPS))
                        if i == 6:
                            act.wait_ge(qkT_done, l * 5 + 4)
                        for t in range(TT):
                            if t == 0:
                                act.wait_ge(proj_done, l * PROJ_CHUNKS + i + 1)
                            else:
                                unit_used(act, l, M_AT, m - 1)
                            src = bank[PROJ[i % 2][t]]
                            if i >= 8:
                                g0 = (i - 8) * NB
                                act.activation(gates[:, t, g0:g0 + NB], src[:, :], ACT.Tanh,
                                               scale=half_rstd[:, t:t + 1]).then_inc(gates_done, 1)
                                continue
                            w = NB
                            if i in (3, 4, 7):
                                v0 = {3: 0, 4: NB, 7: DIL_W}[i]
                                w = DIL_W - NB if i == 4 else NB
                                dst = v[:, t, v0:v0 + w]
                            else:
                                dst = qk_raw[:, t, :]
                            act.activation(dst, src[:, 0:w], ACT.Copy, scale=rstd[:, t:t + 1]).then_inc(proj_read, 1)
                    p = step_pair(m)
                    if p is not None:
                        for hh in range(2):
                            h = 2 * p + hh
                            act.wait_ge(neg_top_done, l * HEADS + h + 1)
                            for t in range(TT):
                                part = probs[:, hh, t, 0:keys(h)]
                                e = act.activation(part, part, ACT.Exp,
                                                   bias=neg_top[:, h, t:t + 1], accum_out=den[:, h, t:t + 1])
                            e.then_inc(exp_done, 1)
                    for j, i in enumerate(QK_CHUNKS):
                        if m == chunk_steps(i)[-1] + 2:
                            act.wait_ge(qkT_done, l * 5 + j + 1)
                            for s in range(2):
                                ft = bank[PROJ[i % 2][s]][:, :].rearrange("p (f s) -> p f s", f=2)
                                if i < GROUPS:
                                    dst = (qT, kT)[s][:, 2 * i:2 * i + 2, :]
                                else:
                                    at = DIL_PAIRS + 2 * s
                                    dst = (qT, kT)[i - 5][:, at:at + 2, :]
                                is_q = (i < GROUPS and s == 0) or i == 5
                                if i == 5:
                                    dst = dst.rearrange("p f (j r) -> p f r j", r=STRIDE)
                                    ft = ft.rearrange("p f (r j) -> p f r j", r=STRIDE)
                                act.activation(dst, ft, ACT.Copy, scale=HD ** -0.5 if is_q else 1.0).then_inc(qkT_read, 1)
                    if m == pair_step(DIL_PAIRS - 1) + 1:
                        act.wait_ge(mix_exp_in, l + 1)
                        act.activation(mix_e[:, :, :], mix_d[:, :, :], ACT.Exp).then_inc(mix_exp, 1)
                    if m == Y_AT:
                        for j in range(3):
                            act.wait_ge(yT_done, l * 3 + j + 1)
                            dst, src = yT_parts(yT_hi, j)
                            act.activation(dst, src, ACT.Copy).then_inc(yT_hi_done, 1)
                    if m == O_AT - 1:
                        for g, (t, n) in enumerate(HALF_MAJOR):
                            act.wait_ge(mT_done, l * 4 + g + 1)
                            act.activation(a_hi[:, 4 * n:4 * n + 4, t * P:(t + 1) * P],
                                           bank[MT[g % 2]][:, :].rearrange("p (k s) -> p k s", k=4),
                                           ACT.Copy).then_inc(mT_hi, 1)

            hi(0, F1_AT, 0)
            act.dma_start(cst[:, 0:C_IDENT], consts[:, 0:C_IDENT]).then_inc(consts_loaded, 16)
            hi(0, F1_AT, 1)
            for t in range(TT):
                act.wait_ge(x_loaded[t], 16 * P // RUN)
            with act.Fori(0, DEPTH) as l:
                feed_forward(l, 0, F1_AT)
                mixer(l)
                feed_forward(l, 1, F2_AT)
            for t in range(TT):
                sum_squares(DEPTH * PHASES, t)

        @block.vector
        def _(dve):
            for i in range(2 * RING):
                dve.memset(credits[:, i:i + 1], 0.0).then_inc((lo_done, split_free)[i % 2], 1)

            def lo(l, at, u, c=None):
                slot = (at + u) % RING
                n = l * L_UNITS + at + u
                if c is not None:
                    n = n + c * 3
                dve.wait_ge(hi_done, n + 1)
                dve.tensor_tensor(w_lo[slot][:, :], raw[slot][:, :], w_hi[slot][:, :].bitcast(F32),
                                  ALU.subtract).then_inc(lo_done, 1)

            def update(l, ph, end, g):
                t, n = GROUP4[g]
                k = (ph - 1) * 4 + g + 1
                if g < 3:
                    dve.wait_ge(acc_done, (ph - 1) * 3 + g + 1)
                else:
                    unit_used(dve, l, end, -1)
                part = x[:, t, n * NB:(n + 1) * NB]
                dve.scalar_tensor_tensor(part, bank[ACC[t][n]][:, :], 0.5, part, ALU.mult, ALU.add).then_inc(x_updated, 1)
                return k

            def scaled(ph, g, updated=None):
                t, n = GROUP4[g]
                if updated is not None:
                    dve.wait_ge(x_updated, updated)
                dve.tensor_tensor(xg[:, t, n * NB:(n + 1) * NB], x[:, t, n * NB:(n + 1) * NB],
                                  gain[:, n * NB:(n + 1) * NB], ALU.mult).then_inc(xg_ready, 1)

            def transposed_lo(ph, g):
                t, n = GROUP4[g]
                dve.wait_ge(xT_hi, ph * 4 + g + 1)
                dve.tensor_tensor(a_lo[:, 4 * n:4 * n + 4, t * P:(t + 1) * P],
                                  bank[TR[g % 2]][:, :].rearrange("p (k s) -> p k s", k=4),
                                  a_hi[:, 4 * n:4 * n + 4, t * P:(t + 1) * P].bitcast(F32),
                                  ALU.subtract).then_inc(xT_lo, 1)

            def input_groups(l, ph, at, turned):
                dve.wait_ge(gain_loaded, ph * 16 + 16)
                for g in range(4):
                    scaled(ph, g, update(l, ph, at, g))
                    if turned and g >= 1:
                        transposed_lo(ph, g - 1)
                if turned:
                    transposed_lo(ph, 3)

            def next_lo(l, f, at, u):
                if f == 0:
                    lo(l, at, F_UNITS + u)
                else:
                    with dve.If(DEPTH - 1 - l):
                        lo(l, at, F_UNITS + u)

            def feed_forward(l, f, at):
                ph = l * PHASES + 2 * f
                ff = l * 2 + f
                if f == 0:
                    for g in range(4):
                        transposed_lo(ph, g)
                else:
                    input_groups(l, ph, at, True)
                lo(l, at, 2)
                dve.wait_ge(rstd_ready, ph + 1)

                def hide(c):
                    for t in range(TT):
                        k = ff * 2 * CHUNKS + c * 2 + t + 1
                        dve.wait_ge(tanh_done, k)
                        dve.scalar_tensor_tensor(gated[:, t, :], tanh_g[:, t, :], 1.0, bank[UP[t]][:, 0:FC],
                                                 ALU.add, ALU.mult).then_inc(gated_done, 1)
                        dve.wait_ge(gated_done, k)
                        dve.scalar_tensor_tensor(hidden[:, t, :], gated[:, t, :], half_rstd2[:, t:t + 1],
                                                 bank[UP[t]][:, FC:2 * FC], ALU.mult, ALU.mult).then_inc(hidden_done, 1)

                def hT_lower(c):
                    for t in range(TT):
                        toks = slice(t * P, (t + 1) * P)
                        dve.wait_ge(hT_hi_done, ff * 2 * CHUNKS + c * 2 + t + 1)
                        dve.tensor_tensor(hT_lo[:, :, toks], bank[HT[t]][:, 0:2 * P].rearrange("p (k s) -> p k s", k=2),
                                          hT_hi[:, :, toks].bitcast(F32), ALU.subtract).then_inc(hT_lo_done, 1)

                hide(0)
                with dve.Fori(1, CHUNKS) as c:
                    lo(l, at, 0, c)
                    lo(l, at, 1, c)
                    hT_lower(c - 1)
                    lo(l, at, 2, c)
                    hide(c)
                next_lo(l, f, at, 0)
                hT_lower(CHUNKS - 1)
                next_lo(l, f, at, 1)

            def rope(l, i):
                heads = qk_raw[:, :, :].rearrange("p t (h s d) -> p t h s d", h=8, s=2)
                turned = qk_rot.rearrange("p t (h s d) -> p t h s d", h=8, s=2)
                c = cos.unsqueeze(2).to_broadcast([P, TT, 8, HALF])
                s = sin.unsqueeze(2).to_broadcast([P, TT, 8, HALF])
                dve.wait_ge(proj_read, l * 16 + 2 * i + 2)
                if i >= 1:
                    dve.wait_ge(qkT_done, l * 5 + i)
                dve.tensor_tensor(rope_tmp[:, 0], heads[:, :, :, 0, :], c, ALU.mult).then_inc(rope_dve_part, 1)
                dve.tensor_tensor(rope_tmp[:, 1], heads[:, :, :, 1, :], s, ALU.mult).then_inc(rope_dve_part, 1)
                dve.wait_ge(rope_dve_part, l * 6 + 2 * i + 2)
                dve.tensor_tensor(turned[:, :, :, 0, :], rope_tmp[:, 0], rope_tmp[:, 1], ALU.subtract).then_inc(rope_dve, 1)

            def probs_turned(l, h):
                dve.wait_ge(probsT_done, l * HEADS + h + 1)
                if h >= 2:
                    dve.wait_ge(pv_done, l * HEADS + h - 1)
                kts = keys(h) // P
                dve.tensor_copy(probsT[:, h % 2, 0:kts, :],
                                bank[PT][:, 0:kts * SEQ].rearrange("p (k q) -> p k q", k=kts)).then_inc(probsT_read, 1)

            def masked(l, h):
                hh = h % 2
                dve.wait_ge(scores_done, l * HEADS + h + 1)
                if h >= 2:
                    dve.wait_ge(probsT_done, l * HEADS + h - 1)
                dve.memset(wait_carrier[:, :], 0.0)
                for t in range(TT):
                    sc = bank[SC[hh]][:, t * SEQ:t * SEQ + keys(h)]
                    to = probs[:, hh, t, 0:keys(h)]
                    if h < GROUP_HEADS:
                        more = near_mask[:, t, :]
                    elif h < DIL_HEADS:
                        more = block_mask[:, h // GROUP_HEADS - 1, :]
                    else:
                        more = bias[:, h - DIL_HEADS, 2 - 2 * t:6 - 2 * t, :].rearrange("p g (j r) -> p r (g j)", r=STRIDE)
                        sc = sc.rearrange("p (r j) -> p r j", r=STRIDE)
                        to = to.rearrange("p (r j) -> p r j", r=STRIDE)
                    r = dve.tensor_tensor_reduce(to, sc, more, 1.0, -3.0e38, ALU.add, ALU.max, top[:, h, t:t + 1])
                r.then_inc(scores_read, 1)
                dve.wait_ge(scores_read, l * HEADS + h + 1)
                dve.tensor_scalar(neg_top[:, h, :], top[:, h, :], -1.0, None, ALU.mult).then_inc(neg_top_done, 1)

            def products_read(l, p):
                src = bank[OB][:, 0:2 * TT * HD].rearrange("p (h t d) -> p h t d", h=2, t=TT)
                if p < DIL_PAIRS:
                    dve.wait_ge(pv_done, l * HEADS + 2 * p + 2)
                    dve.tensor_copy(o_dil[:, 2 * p:2 * p + 2, :, :], src).then_inc(o_read, 1)
                    return
                j = p - DIL_PAIRS
                dve.reciprocal(rden[:, :, :], den[:, 2 * p:2 * p + 2, :]).then_inc(rden_done, 1)
                dve.wait_ge(rden_done, l * (PAIRS - DIL_PAIRS) + j + 1)
                dve.wait_ge(pv_done, l * HEADS + 2 * p + 2)
                at = GROUP_HEADS * HD + 2 * j * HD
                dst = y[:, :, at:at + 2 * HD].rearrange("p t (h d) -> p h t d", h=2)
                dve.tensor_tensor(dst, src, rden[:, :, :].unsqueeze(3).to_broadcast([P, 2, TT, HD]),
                                  ALU.mult).then_inc(o_read, 1)

            def mix_weights(l):
                n = [0]
                tops = top[:, 0:DIL_HEADS, :].rearrange("p (g h) t -> p g (h t)", g=GROUPS)
                dens = den[:, 0:DIL_HEADS, :].rearrange("p (g h) t -> p g (h t)", g=GROUPS)

                def chained(ins):
                    ins.then_inc(mix_chain, 1)
                    n[0] += 1
                    dve.wait_ge(mix_chain, l * 6 + n[0])
                peak = mix[:, 1, :]
                chained(dve.tensor_tensor(mix[:, 0, :], tops[:, 0, :], tops[:, 1, :], ALU.max))
                chained(dve.tensor_tensor(peak, mix[:, 0, :], tops[:, 2, :], ALU.max))
                dve.tensor_tensor(mix_d[:, :, :], tops, peak.unsqueeze(1).to_broadcast([P, GROUPS, GROUP_HEADS * TT]),
                                  ALU.subtract).then_inc(mix_exp_in, 1)
                dve.wait_ge(mix_exp, l + 1)
                chained(dve.tensor_tensor(mix_d[:, :, :], mix_e[:, :, :], dens, ALU.mult))
                chained(dve.tensor_tensor(mix[:, 2, :], mix_d[:, 0, :], mix_d[:, 1, :], ALU.add))
                chained(dve.tensor_tensor(mix[:, 3, :], mix[:, 2, :], mix_d[:, 2, :], ALU.add))
                chained(dve.reciprocal(mix[:, 4, :], mix[:, 3, :]))
                dve.tensor_tensor(mix_d[:, :, :], mix_e[:, :, :],
                                  mix[:, 4, :].unsqueeze(1).to_broadcast([P, GROUPS, GROUP_HEADS * TT]),
                                  ALU.mult).then_inc(mix_ready, 1)

            def mixer(l):
                ph = l * PHASES + 1
                input_groups(l, ph, M_AT, True)
                dve.wait_ge(consts_loaded, 16)
                for m in range(M_UNITS):
                    p = step_pair(m)
                    before = step_pair(m - 1)
                    for hh in range(2):
                        if before is not None:
                            probs_turned(l, 2 * before + hh)
                        if p is not None:
                            if p == DIL_PAIRS and hh == 0:
                                dve.wait_ge(bias_ready, l + 1)
                            masked(l, 2 * p + hh)
                    lo(l, M_AT, m + 2)
                    if m in (2, 4, 6):
                        rope(l, m // 2 - 1)
                    if before is not None:
                        products_read(l, before)
                    if before == DIL_PAIRS - 1:
                        mix_weights(l)
                    if m == Y_AT:
                        for j in range(3):
                            dve.wait_ge(yT_hi_done, l * 3 + j + 1)
                            dst, src = yT_parts(yT_lo, j)
                            upper, _ = yT_parts(yT_hi, j)
                            dve.tensor_tensor(dst, src, upper.bitcast(F32), ALU.subtract).then_inc(yT_lo_done, 1)
                    if m == BA_AT:
                        dve.wait_ge(gates_done, l * 8 + 8)
                        for g, (t, n) in enumerate(GROUP4):
                            if g < 3:
                                dve.wait_ge(a_done, l * 3 + g + 1)
                            else:
                                unit_used(dve, l, M_AT, BA_AT)
                            dve.scalar_tensor_tensor(merged[:, t, n * NB:(n + 1) * NB], gates[:, t, n * NB:(n + 1) * NB], 1.0,
                                                     bank[BANK_A[t][n]][:, :], ALU.add, ALU.mult).then_inc(a_read, 1)
                    if m == O_AT - 1:
                        dve.wait_ge(a_read, l * 4 + 4)
                        for g, (t, n) in enumerate(HALF_MAJOR):
                            if g < 3:
                                dve.wait_ge(b_done, l * 3 + g + 1)
                            else:
                                unit_used(dve, l, M_AT, O_AT - 1)
                            if g >= 1:
                                dve.wait_ge(merged_done, l * 4 + g)
                            dve.scalar_tensor_tensor(from_b, gates[:, t, D + n * NB:D + (n + 1) * NB], 1.0,
                                                     bank[BANK_B[t][n]][:, :], ALU.add, ALU.mult).then_inc(b_read, 1)
                            dve.wait_ge(b_read, l * 4 + g + 1)
                            part = merged[:, t, n * NB:(n + 1) * NB]
                            dve.tensor_tensor(part, part, from_b, ALU.add).then_inc(merged_done, 1)
                            if g >= 1:
                                merged_lo(l, g - 1)
                        merged_lo(l, 3)

            def merged_lo(l, g):
                t, n = HALF_MAJOR[g]
                dve.wait_ge(mT_hi, l * 4 + g + 1)
                dve.tensor_tensor(a_lo[:, 4 * n:4 * n + 4, t * P:(t + 1) * P],
                                  bank[MT[g % 2]][:, :].rearrange("p (k s) -> p k s", k=4),
                                  a_hi[:, 4 * n:4 * n + 4, t * P:(t + 1) * P].bitcast(F32),
                                  ALU.subtract).then_inc(mT_lo, 1)

            dve.wait_ge(gain_loaded, 16)
            for g, (t, n) in enumerate(GROUP4):
                if n == 0:
                    dve.wait_ge(x_loaded[t], 16 * P // RUN)
                scaled(0, g)
            lo(0, F1_AT, 0)
            lo(0, F1_AT, 1)
            with dve.Fori(0, DEPTH) as l:
                feed_forward(l, 0, F1_AT)
                mixer(l)
                feed_forward(l, 1, F2_AT)
                input_groups(l, l * PHASES + PHASES, L_UNITS, False)
            dve.wait_ge(rstd_ready, DEPTH * PHASES + 1)
            for t in range(TT):
                dve.wait_ge(xg_ready, DEPTH * PHASES * 4 + 2 * t + 2)
                dve.tensor_scalar(xg[:, t, :], xg[:, t, :], rstd[:, t:t + 1], None, ALU.mult).then_inc(result_ready, 1)

        @block.tensor
        def _(pe):
            def product(dst, s_hi, s_lo, m_hi, m_lo, start, stop):
                pe.matmul(dst, s_hi, m_hi, start=start, stop=False)
                pe.matmul(dst, s_hi, m_lo, start=False, stop=False)
                return pe.matmul(dst, s_lo, m_hi, start=False, stop=stop)

            def split_ready(l, at, u, c=None):
                n = l * L_UNITS + at + u
                if c is not None:
                    n = n + c * 3
                pe.wait_ge(lo_done, n + 1 + RING)

            def cols(slot, t, a, dst, start, stop, js=range(4), nk=4):
                w = UNIT // nk
                for j in js:
                    k = nk * a + j
                    mm = product(dst[:, 0:w], a_hi[:, k, t * P:(t + 1) * P], a_lo[:, k, t * P:(t + 1) * P],
                                 w_hi[slot][:, j * w:(j + 1) * w], w_lo[slot][:, j * w:(j + 1) * w],
                                 start and j == 0, stop and j == nk - 1)
                return mm

            def rows(slot, s_hi, s_lo, k0, t, n, dst, start, stop):
                for j in range(2):
                    at = j * D + n * NB
                    mm = product(dst[:, :], s_hi[:, k0 + j, t * P:(t + 1) * P], s_lo[:, k0 + j, t * P:(t + 1) * P],
                                 w_hi[slot][:, at:at + NB], w_lo[slot][:, at:at + NB], start and j == 0, stop and j == 1)
                return mm

            def input_transposes(ph, gs):
                for g in gs:
                    t, n = GROUP4[g]
                    pe.wait_ge(xg_ready, ph * 4 + g + 1)
                    if g >= 2:
                        pe.wait_ge(xT_lo, ph * 4 + g - 1)
                    for j in range(4):
                        c = n * NB + j * P
                        tr = pe.transpose(bank[TR[g % 2]][:, j * P:(j + 1) * P], xg[:, t, c:c + P], ident)
                    tr.then_inc(xT_done, 1)

            def feed_forward(l, f, at):
                ph = l * PHASES + 2 * f
                ff = l * 2 + f

                def up(c, a, t, slot):
                    mm = cols(slot, t, a, bank[UP[t]], a == 0, a == 1)
                    if t == 1:
                        mm.then_inc(split_free, 1)
                    elif a == 1:
                        mm.then_inc(up_done, 1)

                def turn(c):
                    for t in range(TT):
                        pe.wait_ge(hidden_done, ff * 2 * CHUNKS + c * 2 + t + 1)
                        for j in range(2):
                            tr = pe.transpose(bank[HT[t]][:, j * P:(j + 1) * P],
                                              hidden[:, t, j * P:(j + 1) * P], ident)
                        tr.then_inc(hT_done, 1)

                def down(c, slot, start, stop):
                    for g, (t, n) in enumerate(GROUP4):
                        if n == 0:
                            pe.wait_ge(hT_lo_done, ff * 2 * CHUNKS + c * 2 + t + 1)
                        mm = rows(slot, hT_hi, hT_lo, 0, t, n, bank[ACC[t][n]], start, stop)
                        if g == 3:
                            mm.then_inc(split_free, 1)
                        elif stop:
                            mm.then_inc(acc_done, 1)

                input_transposes(ph, (0, 1))
                split_ready(l, at, 0)
                pe.wait_ge(xT_lo, ph * 4 + 1)
                up(0, 0, 0, 0)
                input_transposes(ph, (2,))
                split_ready(l, at, 1)
                pe.wait_ge(xT_lo, ph * 4 + 2)
                up(0, 1, 0, 1)
                input_transposes(ph, (3,))
                for a in range(2):
                    pe.wait_ge(xT_lo, ph * 4 + 3 + a)
                    up(0, a, 1, a)

                def chunk(c, first):
                    split_ready(l, at, -1, c)
                    for t in range(TT):
                        pe.wait_ge(hidden_done, ff * 2 * CHUNKS + (c - 1) * 2 + t + 1)
                        up(c, 0, t, 2)
                    turn(c - 1)
                    split_ready(l, at, 0, c)
                    for t in range(TT):
                        up(c, 1, t, 0)
                    split_ready(l, at, 1, c)
                    down(c - 1, 1, first, False)

                chunk(1, True)
                with pe.Fori(2, CHUNKS) as c:
                    chunk(c, False)
                turn(CHUNKS - 1)
                split_ready(l, at, F_UNITS - 1)
                down(CHUNKS - 1, 2, False, True)

            def qk_transposes(l, j, i):
                if i < GROUPS:
                    pe.wait_ge(rope_dve, l * GROUPS + i + 1)
                    pe.wait_ge(rope_pool, l * GROUPS + i + 1)
                    src = qk_rot
                else:
                    pe.wait_ge(proj_read, l * 16 + 2 * i + 2)
                    src = qk_raw
                for f in range(4):
                    for t in range(TT):
                        at = (f % 2) * SEQ + t * P
                        tr = pe.transpose(bank[PROJ[i % 2][f // 2]][:, at:at + P], src[:, t, f * P:(f + 1) * P], ident)
                tr.then_inc(qkT_done, 1)

            def scores(l, h):
                p, hh = h // 2, h % 2
                rows_ = slice(hh * HD, (hh + 1) * HD)
                for t in range(TT):
                    k0 = t * P if keys(h) == P else 0
                    mm = pe.matmul(bank[SC[hh]][:, t * SEQ:t * SEQ + keys(h)], qT[rows_, p, t * P:(t + 1) * P],
                                   kT[rows_, p, k0:k0 + keys(h)], start=True, stop=True)
                mm.then_inc(scores_done, 1)

            def turn_probs(l, h):
                pe.wait_ge(exp_done, l * HEADS + h + 1)
                if h >= 1:
                    pe.wait_ge(probsT_read, l * HEADS + h)
                for k in range(keys(h) // P):
                    for t in range(TT):
                        part = probs[:, h % 2, t, k * P:(k + 1) * P]
                        tr = pe.transpose(bank[PT][:, k * SEQ + t * P:k * SEQ + (t + 1) * P], part, ident)
                tr.then_inc(probsT_done, 1)

            def times_v(l, h):
                p, hh = h // 2, h % 2
                pe.wait_ge(probsT_read, l * HEADS + h + 1)
                if hh == 0:
                    if p >= 1:
                        pe.wait_ge(o_read, l * PAIRS + p)
                    pe.wait_ge(proj_read, l * 16 + (10 if p < DIL_PAIRS else 16))
                for t in range(TT):
                    kts = range(TT) if keys(h) == SEQ else (t,)
                    for k in kts:
                        at = (hh * TT + t) * HD
                        mm = pe.matmul(bank[OB][:, at:at + HD], probsT[:, hh, k - kts[0], t * P:(t + 1) * P],
                                       v[:, k, h * HD:(h + 1) * HD], start=k == kts[0], stop=k == kts[-1])
                mm.then_inc(pv_done, 1)

            def mixer(l):
                ph = l * PHASES + 1
                input_transposes(ph, (0, 1))
                for t in range(TT):
                    for a in range(2):
                        split_ready(l, M_AT, a)
                        pe.wait_ge(xT_lo, ph * 4 + 2 * t + a + 1)
                        mm = cols((M_AT + a) % RING, t, a, bank[PROJ[0][t]], a == 0, a == 1)
                        if t == 1:
                            mm.then_inc(split_free, 1)
                        else:
                            if a == 1:
                                mm.then_inc(proj_done, 1)
                            input_transposes(ph, (2 + a,))
                for m in range(2, O_AT):
                    slot = (M_AT + m) % RING
                    p, before = step_pair(m), step_pair(m - 1)
                    if before is not None:
                        turn_probs(l, 2 * before)
                    if p is not None:
                        pe.wait_ge(qkT_read, l * 10 + (2 * (p // 2) + 2 if p < DIL_PAIRS else 10))
                        if p >= 1:
                            pe.wait_ge(scores_read, l * HEADS + 2 * p)
                        scores(l, 2 * p)
                        scores(l, 2 * p + 1)
                    if m == Y_AT:
                        pe.wait_ge(y_dil_done, l + 1)
                        pe.wait_ge(o_read, l * PAIRS + PAIRS)
                        for j in range(3):
                            for f in range(2):
                                for t in range(TT):
                                    at = f * SEQ + t * P
                                    c = (2 * j + f) * P
                                    tr = pe.transpose(bank[YT[j]][:, at:at + P], y[:, t, c:c + P], ident)
                            tr.then_inc(yT_done, 1)
                    i, a = step_chunk(m)
                    if i is not None:
                        if a == 0 and i >= 2:
                            if i - 2 in QK_CHUNKS:
                                pe.wait_ge(qkT_read, l * 10 + 2 * QK_CHUNKS.index(i - 2) + 2)
                            elif i - 2 < 8:
                                pe.wait_ge(proj_read, l * 16 + 2 * (i - 2) + 2)
                            else:
                                pe.wait_ge(gates_done, l * 8 + 2 * (i - 10) + 2)
                        split_ready(l, M_AT, m)
                        last = a == len(chunk_steps(i)) - 1
                        nk = 8 if i == 4 else 4
                        for t in range(TT):
                            if t == 1:
                                for j, turned in enumerate(QK_CHUNKS):
                                    if m == chunk_steps(turned)[-1] + 2:
                                        qk_transposes(l, j, turned)
                            for q in range(2):
                                js = range(q * nk // 2, (q + 1) * nk // 2)
                                mm = cols(slot, t, a, bank[PROJ[i % 2][t]], a == 0, last, js, nk)
                                if q == 1 and t == 1:
                                    mm.then_inc(split_free, 1)
                                elif q == 1 and last:
                                    mm.then_inc(proj_done, 1)
                                if before is not None:
                                    if t == 0 and q == 0:
                                        turn_probs(l, 2 * before + 1)
                                    if t == 0 and q == 1:
                                        times_v(l, 2 * before)
                                    if t == 1 and q == 0:
                                        times_v(l, 2 * before + 1)
                    elif m == BA_AT:
                        split_ready(l, M_AT, m)
                        pe.wait_ge(yT_lo_done, l * 3 + 3)
                        pe.wait_ge(gates_done, l * 8 + 6)
                        for g, (t, n) in enumerate(GROUP4):
                            mm = rows(slot, yT_hi, yT_lo, 0, t, n, bank[BANK_A[t][n]], True, True)
                            mm.then_inc(a_done if g < 3 else split_free, 1)
                    else:
                        split_ready(l, M_AT, m)
                        if m == BB_AT:
                            pe.wait_ge(gates_done, l * 8 + 8)
                        last = m == BB_AT + 1
                        for g, (t, n) in enumerate(HALF_MAJOR):
                            mm = rows(slot, yT_hi, yT_lo, 2 * (m - BB_AT) + 2, t, n, bank[BANK_B[t][n]], not last, last)
                            if g == 3:
                                mm.then_inc(split_free, 1)
                            elif last:
                                mm.then_inc(b_done, 1)

                def merged_transposes(gs):
                    for g in gs:
                        t, n = HALF_MAJOR[g]
                        pe.wait_ge(merged_done, l * 4 + g + 1)
                        if g >= 2:
                            pe.wait_ge(mT_lo, l * 4 + g - 1)
                        for j in range(4):
                            c = n * NB + j * P
                            tr = pe.transpose(bank[MT[g % 2]][:, j * P:(j + 1) * P], merged[:, t, c:c + P], ident)
                        tr.then_inc(mT_done, 1)

                merged_transposes((0, 1))
                for j in range(4):
                    m = O_AT + j
                    split_ready(l, M_AT, m)
                    if j == 2:
                        pe.wait_ge(mT_lo, l * 4 + 4)
                    for g, (t, n) in enumerate(GROUP4):
                        if j == 0 and n == 0:
                            pe.wait_ge(mT_lo, l * 4 + t + 1)
                        mm = rows((M_AT + m) % RING, a_hi, a_lo, 2 * j, t, n, bank[ACC[t][n]], j == 0, j == 3)
                        if g == 3:
                            mm.then_inc(split_free, 1)
                        elif j == 3:
                            mm.then_inc(acc_done, 1)
                    if j == 0:
                        merged_transposes((2, 3))

            pe.wait_ge(ident_loaded, 16)
            with pe.Fori(0, DEPTH) as l:
                feed_forward(l, 0, F1_AT)
                mixer(l)
                feed_forward(l, 1, F2_AT)


_INS = ["ffn1_w_up", "ffn1_w_down", "ffn2_w_up", "ffn2_w_down", "w_in", "na_rel_bias", "w_branch_a", "w_branch_b", "w_out"]


def _constants():
    pos = np.arange(SEQ).reshape(RUN, STRIDE).T.reshape(-1)
    rel = pos[None, :] - pos[:, None]
    parts = []
    for g, (window, dilation) in enumerate(DIL_PATTERNS):
        half = window // 2 // dilation
        ok = (rel % dilation == 0) & (np.abs(rel) <= half * dilation)
        mask = np.where(ok, 0.0, NEG_INF).astype(np.float32)
        if g == 0:
            parts += [mask[t * P:(t + 1) * P] for t in range(TT)]
        else:
            assert mask[:P, P:].max() == mask[P:, :P].max() == NEG_INF and (mask[:P, :P] == mask[P:, P:]).all()
            parts.append(mask[:P, :P])
    qc = np.arange(P) % GRID_W
    low = np.clip(qc - NA_COLS // 2, 0, GRID_W - NA_COLS)[:, None]
    kc = np.arange(GRID_W)[None, :]
    parts.append(np.where((kc >= low) & (kc < low + NA_COLS), 0.0, NEG_INF).astype(np.float32))
    freq = np.float32(10000.0) ** (-np.arange(HALF, dtype=np.float32) / np.float32(HALF))
    angle = pos.astype(np.float32)[:, None] * freq[None, :]
    for table in (np.cos(angle), np.sin(angle)):
        parts += [table[t * P:(t + 1) * P].astype(np.float32) for t in range(TT)]
    parts.append(np.eye(P, dtype=np.float32))
    return np.concatenate(parts, axis=1)


def kernel(**inputs):
    import concourse.bacc as _bacc
    from concourse.bass_utils import run_bass_kernel_spmd as _run

    nc = _bacc.Bacc("TRN2", target_bir_lowering=False, num_devices=1)
    rows = [inputs[name][l] for l in range(DEPTH) for name in ("ffn1_norm", "mix_norm", "ffn2_norm")]
    arrays = {name: np.ascontiguousarray(inputs[name]) for name in _INS}
    arrays["x"] = np.ascontiguousarray(inputs["x"]).reshape(SEQ, D)
    arrays["gains"] = np.stack(rows + [inputs["final_norm"]])
    arrays["consts"] = _constants()
    ap = {name: nc.dram_tensor(f"{name}_dram", a.shape, F32, kind="ExternalInput").ap() for name, a in arrays.items()}
    out = nc.dram_tensor("out_dram", (SEQ, D), F32, kind="ExternalOutput").ap()
    build(nc, ap["x"], ap["gains"], (ap["ffn1_w_up"], ap["ffn2_w_up"]), (ap["ffn1_w_down"], ap["ffn2_w_down"]),
          ap["w_in"], ap["na_rel_bias"], ap["w_branch_a"], ap["w_branch_b"], ap["w_out"], ap["consts"], out)
    r = _run(nc, [{f"{name}_dram": a for name, a in arrays.items()}], core_ids=[0])
    return r.results[0]["out_dram"].reshape(1, SEQ, D)
```

```python
from contextlib import ExitStack

import concourse.bass as bass
import numpy as np
from concourse import mybir

ALU = mybir.AluOpType
ACT = mybir.ActivationFunctionType
F32 = mybir.dt.float32
F32R = mybir.dt.float32r

P = 128
SEQ = 256
TT = SEQ // P
D = 1024
KT = D // P
DEPTH = 2
D_FF = 2816
HD = 64
HALF = HD // 2
DIL_PATTERNS = ((128, 1), (512, 4), (2048, 16))
GROUPS = len(DIL_PATTERNS)
GROUP_HEADS = 4
DIL_HEADS = GROUPS * GROUP_HEADS
NA_HEADS = 8
HEADS = DIL_HEADS + NA_HEADS
GRID_W = 64
NA_COLS = 16
REL_ROWS, REL_COLS = 15, 31
DIL_W = DIL_HEADS * HD
STRIDE = DIL_PATTERNS[1][1]
RUN = SEQ // STRIDE
assert all(d % STRIDE == 0 for _, d in DIL_PATTERNS[1:]) and P % RUN == 0
NA_W = NA_HEADS * HD
NA_AT = 3 * DIL_W
GATE_AT = NA_AT + 3 * NA_W
EPS = 1e-6
NEG_INF = -1e30

NB = 512
UNIT = 2048
RING = 3
FC = 256
CHUNKS = D_FF // FC
F_UNITS = 3 * CHUNKS
M_UNITS = 30
L_UNITS = 2 * F_UNITS + M_UNITS
F1_AT, M_AT, F2_AT = 0, F_UNITS, F_UNITS + M_UNITS
assert F_UNITS % RING == 0 and M_UNITS % RING == 0
PHASES = 3
PAIRS = HEADS // 2
DIL_PAIRS = DIL_HEADS // 2
BIAS_ROWS = 6

V_AT, VC_AT, NQ_AT, G_AT, BA_AT, BB_AT, O_AT = 6, 8, 9, 15, 23, 24, 26
PROJ_CHUNKS = 12
QK_CHUNKS = (0, 1, 2, 5, 6)
Y_AT = 22

C_MASK = 0
C_BLOCK = C_MASK + TT * SEQ
C_NAMASK = C_BLOCK + (GROUPS - 1) * P
C_COS = C_NAMASK + GRID_W
C_SIN = C_COS + TT * HALF
C_IDENT = C_SIN + TT * HALF
C_ALL = C_IDENT + P


def chunk_steps(i):
    if i < 4:
        return (2 * i, 2 * i + 1)
    if i == 4:
        return (VC_AT,)
    return (NQ_AT + 2 * (i - 5), NQ_AT + 2 * (i - 5) + 1)


def step_chunk(m):
    for i in range(PROJ_CHUNKS):
        if m in chunk_steps(i):
            return i, chunk_steps(i).index(m)
    return None, 0


def pair_step(p):
    return NQ_AT + p if p < DIL_PAIRS else G_AT + 1 + p - DIL_PAIRS


def step_pair(m):
    for p in range(PAIRS):
        if pair_step(p) == m:
            return p
    return None


def build(nc, x_in, gains, w_up, w_down, w_in, rel_bias, w_a, w_b, w_out, consts, out):
    bias_rows = nc.dram_tensor("bias_rows", [DEPTH, P, NA_HEADS, BIAS_ROWS, GRID_W], F32, kind="Internal").ap()
    with ExitStack() as ctx:
        def sb(name, shape, dt=F32):
            return ctx.enter_context(nc.sbuf_tensor(name, shape, dt))

        def sem(name):
            return ctx.enter_context(nc.semaphore(name))

        raw = [sb(f"raw{i}", [P, UNIT]) for i in range(RING)]
        w_hi = [sb(f"w_hi{i}", [P, UNIT], F32R) for i in range(RING)]
        w_lo = [sb(f"w_lo{i}", [P, UNIT], F32R) for i in range(RING)]
        x = sb("x", [P, TT, D])
        gain = sb("gain", [P, D])
        a_hi = sb("a_hi", [P, KT, SEQ], F32R)
        a_lo = sb("a_lo", [P, KT, SEQ], F32R)
        qT = sb("qT", [P, PAIRS, SEQ])
        kT = sb("kT", [P, PAIRS, SEQ])
        v = sb("v", [P, TT, HEADS * HD])
        qk_raw = sb("qk_raw", [P, TT, NB])
        gates = sb("gates", [P, TT, 2 * D])
        bias = sb("bias", [P, NA_HEADS, BIAS_ROWS, GRID_W])
        cst = sb("cst", [P, C_ALL])
        hT_hi = sb("hT_hi", [P, 2, SEQ], F32R)
        hT_lo = sb("hT_lo", [P, 2, SEQ], F32R)
        probs = sb("probs", [P, 2, TT, SEQ])
        probsT = sb("probsT", [P, 2, TT, SEQ])
        o_dil = sb("o_dil", [P, DIL_HEADS, TT, HD])
        y = sb("y", [P, TT, GROUP_HEADS * HD + NA_W])
        yT_hi = sb("yT_hi", [P, 6, SEQ], F32R)
        yT_lo = sb("yT_lo", [P, 6, SEQ], F32R)
        top = sb("top", [P, HEADS, TT])
        neg_top = sb("neg_top", [P, HEADS, TT])
        den = sb("den", [P, HEADS, TT])
        rden = sb("rden", [P, 2, TT])
        mix = sb("mix", [P, 5, GROUP_HEADS * TT])
        mix_e = sb("mix_e", [P, GROUPS, GROUP_HEADS * TT])
        mix_d = sb("mix_d", [P, GROUPS, GROUP_HEADS * TT])
        stat = sb("stat", [P, 8, TT])
        wait_carrier = sb("wait_carrier", [P, 1])
        credits = sb("credits", [P, 2 * RING])

        flat_gates = gates[:, :, :].rearrange("p t n -> p (t n)")
        xg = flat_gates[:, 0:TT * D].rearrange("p (t n) -> p t n", t=TT)
        rope_tmp = flat_gates[:, 0:4 * TT * 8 * HALF].rearrange("p (i t h d) -> p i t h d", i=4, t=TT, h=8)
        qk_rot = flat_gates[:, TT * D:TT * D + TT * NB].rearrange("p (t n) -> p t n", t=TT)
        flat_probs = probs[:, :, :, :].rearrange("p a t k -> p (a t k)")
        tanh_g = flat_probs[:, 0:TT * FC].rearrange("p (t n) -> p t n", t=TT)
        gated = flat_probs[:, TT * FC:2 * TT * FC].rearrange("p (t n) -> p t n", t=TT)
        hidden = probsT[:, :, :, :].rearrange("p a t k -> p (a t k)")[:, 0:TT * FC].rearrange("p (t n) -> p t n", t=TT)
        squares = flat_probs
        merged = qT[:, :, :].rearrange("p a b -> p (a b)")[:, 0:TT * D].rearrange("p (t n) -> p t n", t=TT)
        from_b = qk_raw[:, 0, :]

        near_mask = cst[:, C_MASK:C_BLOCK].rearrange("p (t k) -> p t k", t=TT)
        block_mask = cst[:, C_BLOCK:C_NAMASK].rearrange("p (g k) -> p g k", g=GROUPS - 1)
        na_mask = cst[:, C_NAMASK:C_COS]
        cos = cst[:, C_COS:C_SIN].rearrange("p (t d) -> p t d", t=TT)
        sin = cst[:, C_SIN:C_IDENT].rearrange("p (t d) -> p t d", t=TT)
        ident = cst[:, C_IDENT:C_ALL]
        mean_sq4, rstd, half_rstd, half_rstd2, minus_half, eps4 = (stat[:, i, :] for i in range(6))
        half_sums = stat[:, 6:8, :]

        bank = [ctx.enter_context(nc.psum_tensor(f"bank{i}", [P, NB], F32)) for i in range(8)]
        UP = (0, 1)
        TR = (2, 3)
        HT = (2, 3)
        ACC = ((4, 5), (6, 7))
        PROJ = ((0, 1), (4, 5))
        SC = (6, 7)
        PT, OB = 2, 3
        YT = (6, 7, 2)
        BANK_A = ((0, 1), (6, 7))
        BANK_B = ((4, 2), (5, 3))
        MT = (0, 1)

        x_loaded = [sem(f"x_loaded{t}") for t in range(TT)]
        ident_loaded = sem("ident_loaded")
        consts_loaded = sem("consts_loaded")
        first_gain = sem("first_gain")
        gain_loaded = sem("gain_loaded")
        bias_spread = sem("bias_spread")
        bias_loaded = sem("bias_loaded")
        bias_ready = sem("bias_ready")
        raw_arrived = [sem(f"raw_arrived{i}") for i in range(RING)]
        hi_done = sem("hi_done")
        first_half = sem("first_half")
        lo_done = sem("lo_done")
        split_free = sem("split_free")
        x_updated = sem("x_updated")
        xg_ready = sem("xg_ready")
        xT_done = sem("xT_done")
        xT_hi = sem("xT_hi")
        xT_lo = sem("xT_lo")
        squares_done = sem("squares_done")
        pool_chain = sem("pool_chain")
        numbers_set = sem("numbers_set")
        rstd_ready = sem("rstd_ready")
        up_done = sem("up_done")
        tanh_done = sem("tanh_done")
        gated_done = sem("gated_done")
        hidden_done = sem("hidden_done")
        hT_done = sem("hT_done")
        hT_hi_done = sem("hT_hi_done")
        hT_lo_done = sem("hT_lo_done")
        acc_done = sem("acc_done")
        proj_done = sem("proj_done")
        proj_read = sem("proj_read")
        rope_dve = sem("rope_dve")
        rope_dve_part = sem("rope_dve_part")
        rope_pool = sem("rope_pool")
        rope_pool_part = sem("rope_pool_part")
        qkT_done = sem("qkT_done")
        qkT_read = sem("qkT_read")
        scores_done = sem("scores_done")
        scores_read = sem("scores_read")
        neg_top_done = sem("neg_top_done")
        exp_done = sem("exp_done")
        probsT_done = sem("probsT_done")
        probsT_read = sem("probsT_read")
        pv_done = sem("pv_done")
        rden_done = sem("rden_done")
        o_read = sem("o_read")
        mix_chain = sem("mix_chain")
        mix_exp_in = sem("mix_exp_in")
        mix_exp = sem("mix_exp")
        mix_ready = sem("mix_ready")
        mix_part = sem("mix_part")
        y_dil_done = sem("y_dil_done")
        gates_done = sem("gates_done")
        yT_done = sem("yT_done")
        yT_hi_done = sem("yT_hi_done")
        yT_lo_done = sem("yT_lo_done")
        a_done = sem("a_done")
        a_read = sem("a_read")
        b_done = sem("b_done")
        b_read = sem("b_read")
        merged_done = sem("merged_done")
        mT_done = sem("mT_done")
        mT_hi = sem("mT_hi")
        mT_lo = sem("mT_lo")
        result_ready = sem("result_ready")
        out_written = sem("out_written")

        GROUP4 = ((0, 0), (1, 0), (0, 1), (1, 1))

        def residues(rows):
            return rows.rearrange("(j r) d -> r j d", r=STRIDE)

        def stream_part(tile, r):
            at = r * RUN % P
            return tile[at:at + RUN, r * RUN // P, :]

        def yT_parts(yT, j):
            dst = yT[:, 2 * j:2 * j + 2, :]
            src = bank[YT[j]][:, :].rearrange("p (f s) -> p f s", f=2)
            if j == 0:
                return dst, src
            return dst.rearrange("p f (r j) -> p f r j", r=STRIDE), src.rearrange("p f (j r) -> p f r j", r=STRIDE)

        def keys(h):
            return P if GROUP_HEADS <= h < DIL_HEADS else SEQ

        def unit_used(eng, l, at, u, c=None):
            n = l * L_UNITS + at + u + 1 + RING
            eng.wait_ge(split_free, n if c is None else n + c * 3)

        block = ctx.enter_context(nc.Block())

        @block.sync
        def _(sp):
            def unit(n, slot, parts):
                sp.wait_ge(lo_done, n + 1)
                for dst, src in parts(raw[slot]):
                    sp.dma_start(dst, src).then_inc(raw_arrived[slot], 16)

            def load_gain(row):
                sp.dma_start(gain[:, :], gains[row, :].partition_broadcast(P)).then_inc(gain_loaded, 16)

            def up_unit(f, l, c, a):
                src = w_up[f].rearrange("l (k p) n -> l p k n", p=P)

                def parts(place):
                    to = place[:, :].rearrange("p (k n) -> p k n", n=2 * FC)
                    for g in range(2):
                        cols = src[:, :, 4 * a:4 * a + 4, g * D_FF:(g + 1) * D_FF]
                        yield to[:, :, g * FC:(g + 1) * FC], cols[l, :, :, bass.ts(c, FC)]
                return parts

            def rows_unit(w, l, k0):
                src = w.rearrange("l (k p) n -> l p k n", p=P)

                def parts(place):
                    for j in range(2):
                        yield place[:, j * D:(j + 1) * D], src[l, :, k0 + j, :]
                return parts

            def down_unit(f, l, c):
                rows = w_down[f].rearrange("l (k p) n -> l k p n", p=P)

                def parts(place):
                    for j in range(2):
                        yield place[:, j * D:(j + 1) * D], rows[l, c * 2 + j, :, :]
                return parts

            def cols_unit(l, c0, a):
                src = w_in.rearrange("l (k p) n -> l p k n", p=P)

                def parts(place):
                    to = place[:, :].rearrange("p (k n) -> p k n", n=NB)
                    for j in range(2):
                        k = 4 * a + 2 * j
                        yield to[:, 2 * j:2 * j + 2, :], src[l, :, k:k + 2, c0:c0 + NB]
                return parts

            def qk_unit(l, g, a):
                src = w_in.rearrange("l (k p) n -> l p k n", p=P)
                w = GROUP_HEADS * HD

                def parts(place):
                    to = place[:, :].rearrange("p (k n) -> p k n", n=NB)
                    for j in range(2):
                        c0 = j * DIL_W + g * w
                        yield to[:, :, j * w:(j + 1) * w], src[l, :, 4 * a:4 * a + 4, c0:c0 + w]
                return parts

            def last_v_unit(l):
                src = w_in.rearrange("l (k p) n -> l p k n", p=P)
                c0 = 2 * DIL_W + NB

                def parts(place):
                    to = place[:, :].rearrange("p (k n) -> p k n", n=DIL_W - NB)
                    for j in range(2):
                        yield to[:, 4 * j:4 * j + 4, :], src[l, :, 4 * j:4 * j + 4, c0:NA_AT]
                return parts

            def feed_forward(f, l, at, next_gain):
                n0 = l * L_UNITS + at
                unit(n0, 0, up_unit(f, l, 0, 0))
                unit(n0 + 1, 1, up_unit(f, l, 0, 1))
                with sp.Fori(1, CHUNKS) as c:
                    unit(n0 + c * 3 - 1, 2, up_unit(f, l, c, 0))
                    unit(n0 + c * 3, 0, up_unit(f, l, c, 1))
                    unit(n0 + c * 3 + 1, 1, down_unit(f, l, c - 1))
                load_gain(next_gain)
                unit(n0 + F_UNITS - 1, 2, down_unit(f, l, CHUNKS - 1))

            sp.dma_start(gain[:, 0:NB], gains[0, 0:NB].partition_broadcast(P)).then_inc(first_gain, 16)
            sp.dma_start(ident, consts[:, C_IDENT:C_ALL]).then_inc(ident_loaded, 16)
            with sp.Fori(0, DEPTH) as l:
                feed_forward(0, l, F1_AT, l * PHASES + 1)
                sp.wait_ge(bias_spread, 16 * DEPTH * 2 * BIAS_ROWS)
                sp.dma_start(bias[:, :, :, :].rearrange("p h r k -> p (h r k)"),
                             bias_rows.rearrange("l p h r k -> l p (h r k)")[l, :, :]).then_inc(bias_loaded, 16)
                n0 = l * L_UNITS + M_AT
                m = 0
                for g in range(GROUPS):
                    for a in range(2):
                        unit(n0 + m, m % RING, qk_unit(l, g, a))
                        m += 1
                for a in range(2):
                    unit(n0 + m, m % RING, cols_unit(l, 2 * DIL_W, a))
                    m += 1
                unit(n0 + m, m % RING, last_v_unit(l))
                m += 1
                for i in range(7):
                    for a in range(2):
                        unit(n0 + m, m % RING, cols_unit(l, NA_AT + i * NB, a))
                        m += 1
                unit(n0 + m, m % RING, rows_unit(w_a, l, 0))
                m += 1
                load_gain(l * PHASES + 2)
                for k0 in (0, 2):
                    unit(n0 + m, m % RING, rows_unit(w_b, l, k0))
                    m += 1
                for k0 in range(0, KT, 2):
                    unit(n0 + m, m % RING, rows_unit(w_out, l, k0))
                    m += 1
                feed_forward(1, l, F2_AT, l * PHASES + 3)
            for r in range(STRIDE):
                sp.wait_ge(result_ready, r * RUN // P + 1)
                sp.dma_start(residues(out)[r, :, :], stream_part(xg, r)).then_inc(out_written, 16)
            sp.wait_ge(out_written, 16 * STRIDE)

        @block.gpsimd
        def _(pool):
            for tile, number in ((minus_half, -0.5), (eps4, 4 * EPS)):
                pool.memset(tile, number).then_inc(numbers_set, 1)
            def norm_factors(ph):
                pool.wait_ge(squares_done, ph * 4 + 4)
                pool.tensor_tensor(mean_sq4, half_sums[:, 0, :], half_sums[:, 1, :], ALU.add).then_inc(pool_chain, 1)
                pool.wait_ge(pool_chain, ph * 4 + 1)
                pool.tensor_tensor(mean_sq4, mean_sq4, eps4, ALU.add).then_inc(pool_chain, 1)
                pool.wait_ge(pool_chain, ph * 4 + 2)
                pool.tensor_tensor(half_rstd, mean_sq4, minus_half, ALU.pow).then_inc(pool_chain, 1)
                pool.wait_ge(pool_chain, ph * 4 + 3)
                pool.tensor_tensor(rstd, half_rstd, half_rstd, ALU.add).then_inc(pool_chain, 1)
                pool.wait_ge(pool_chain, ph * 4 + 4)
                pool.tensor_tensor(half_rstd2, rstd, half_rstd, ALU.mult).then_inc(rstd_ready, 1)

            def rope(l, i):
                heads = qk_raw[:, :, :].rearrange("p t (h s d) -> p t h s d", h=8, s=2)
                turned = qk_rot.rearrange("p t (h s d) -> p t h s d", h=8, s=2)
                c = cos.unsqueeze(2).to_broadcast([P, TT, 8, HALF])
                s = sin.unsqueeze(2).to_broadcast([P, TT, 8, HALF])
                pool.wait_ge(proj_read, l * 16 + 2 * i + 2)
                if i >= 1:
                    pool.wait_ge(qkT_done, l * 5 + i)
                pool.tensor_tensor(rope_tmp[:, 2], heads[:, :, :, 1, :], c, ALU.mult).then_inc(rope_pool_part, 1)
                pool.tensor_tensor(rope_tmp[:, 3], heads[:, :, :, 0, :], s, ALU.mult).then_inc(rope_pool_part, 1)
                pool.wait_ge(rope_pool_part, l * 6 + 2 * i + 2)
                pool.tensor_tensor(turned[:, :, :, 1, :], rope_tmp[:, 2], rope_tmp[:, 3], ALU.add).then_inc(rope_pool, 1)

            pool.wait_ge(numbers_set, 2)
            norm_factors(0)
            for l in range(DEPTH):
                for a in range(2):
                    for r in range(BIAS_ROWS):
                        at = l * NA_HEADS * REL_ROWS * REL_COLS + (r - 2 - a + 7) * REL_COLS + NA_COLS - 1
                        src = bass.AP(rel_bias.tensor, at, [[REL_ROWS * REL_COLS, NA_HEADS], [-1, GRID_W], [1, GRID_W]])
                        dst = bias_rows[l, GRID_W * a:GRID_W * (a + 1), :, r, :].rearrange("q h k -> h q k")
                        pool.dma_start(dst, src).then_inc(bias_spread, 16)
            pool.wait_ge(consts_loaded, 16)
            with pool.Fori(0, DEPTH) as l:
                pool.wait_ge(bias_loaded, l * 16 + 16)
                rows = bias[:, :, :, :].rearrange("p h r k -> p (h r) k")
                pool.tensor_tensor(rows, rows, na_mask.unsqueeze(1).to_broadcast([P, NA_HEADS * BIAS_ROWS, GRID_W]),
                                   ALU.add).then_inc(bias_ready, 1)
                norm_factors(l * PHASES + 1)
                for i in range(GROUPS):
                    rope(l, i)
                pool.wait_ge(mix_ready, l + 1)
                pool.wait_ge(o_read, l * PAIRS + DIL_PAIRS)
                oh = o_dil[:, :, :, :].rearrange("p h t d -> p (h t) d")
                wts = mix_d[:, :, :].rearrange("p g j -> p (g j)").unsqueeze(2).to_broadcast([P, DIL_HEADS * TT, HD])
                pool.tensor_tensor(oh, oh, wts, ALU.mult).then_inc(mix_part, 1)
                pool.wait_ge(mix_part, l * 2 + 1)
                og = [o_dil[:, g * GROUP_HEADS:(g + 1) * GROUP_HEADS, :, :] for g in range(GROUPS)]
                pool.tensor_tensor(og[0], og[0], og[1], ALU.add).then_inc(mix_part, 1)
                pool.wait_ge(mix_part, l * 2 + 2)
                ya = y[:, :, 0:GROUP_HEADS * HD].rearrange("p t (h d) -> p h t d", h=GROUP_HEADS)
                pool.tensor_tensor(ya, og[0], og[2], ALU.add).then_inc(y_dil_done, 1)
                norm_factors(l * PHASES + 2)
                norm_factors(l * PHASES + 3)

        @block.scalar
        def _(act):
            def load_x(t):
                for r in range(t * P // RUN, (t + 1) * P // RUN):
                    act.dma_start(stream_part(x, r), residues(x_in)[r, :, :]).then_inc(x_loaded[t], 16)

            for t in range(TT):
                load_x(t)
            act.dma_start(gain[:, NB:D], gains[0, NB:D].partition_broadcast(P)).then_inc(gain_loaded, 16)

            def hi(l, at, u, c=None):
                slot = (at + u) % RING
                n = l * L_UNITS + at + u
                turn = l * (L_UNITS // RING) + (at + u) // RING + 1
                if c is not None:
                    n = n + c * 3
                    turn = turn + c
                act.wait_ge(raw_arrived[slot], turn * 32)
                act.wait_ge(split_free, n + 1)
                act.activation(w_hi[slot][:, :], raw[slot][:, :], ACT.Copy).then_inc(hi_done, 1)

            def transposed_hi(ph, g):
                t, n = GROUP4[g]
                act.wait_ge(xT_done, ph * 4 + g + 1)
                act.activation(a_hi[:, 4 * n:4 * n + 4, t * P:(t + 1) * P],
                               bank[TR[g % 2]][:, :].rearrange("p (k s) -> p k s", k=4), ACT.Copy).then_inc(xT_hi, 1)

            def sum_squares(ph, g, last=False):
                t, n = GROUP4[g]
                if last:
                    act.wait_ge(x_updated, ph * 4)
                else:
                    act.wait_ge(xg_ready, ph * 4 + g + 1)
                if g >= 2:
                    act.wait_ge(squares_done, ph * 4 + g - 1)
                act.activation(squares[:, g % 2 * NB:(g % 2 + 1) * NB], x[:, t, n * NB:(n + 1) * NB], ACT.Square, scale=2 * D ** -0.5,
                               accum_out=half_sums[:, n, t:t + 1]).then_inc(squares_done, 1)

            def input_begin(ph):
                sum_squares(ph, 0)
                transposed_hi(ph, 0)
                sum_squares(ph, 1)
                sum_squares(ph, 2)
                transposed_hi(ph, 1)

            def input_end(l, ph, at):
                hi(l, at, 2)
                sum_squares(ph, 3)
                transposed_hi(ph, 2)
                transposed_hi(ph, 3)

            def next_hi(l, f, at, u):
                if f == 0:
                    hi(l, at, F_UNITS + u)
                else:
                    with act.If(DEPTH - 1 - l):
                        hi(l, at, F_UNITS + u)

            def feed_forward(l, f, at):
                ph = l * PHASES + 2 * f
                ff = l * 2 + f
                if f == 1:
                    input_begin(ph)
                input_end(l, ph, at)

                def tanh(c):
                    for t in range(TT):
                        if t == 0:
                            act.wait_ge(up_done, ff * CHUNKS + c + 1)
                        else:
                            unit_used(act, l, at, *((1, None) if isinstance(c, int) and c == 0 else (0, c)))
                        act.activation(tanh_g[:, t, :], bank[UP[t]][:, 0:FC], ACT.Tanh,
                                       scale=half_rstd[:, t:t + 1]).then_inc(tanh_done, 1)

                def hT_upper(c):
                    for t in range(TT):
                        toks = slice(t * P, (t + 1) * P)
                        act.wait_ge(hT_done, ff * 2 * CHUNKS + c * 2 + t + 1)
                        act.activation(hT_hi[:, :, toks], bank[HT[t]][:, 0:2 * P].rearrange("p (k s) -> p k s", k=2),
                                       ACT.Copy).then_inc(hT_hi_done, 1)

                act.wait_ge(rstd_ready, ph + 1)
                tanh(0)
                with act.Fori(1, CHUNKS) as c:
                    hi(l, at, 0, c)
                    hi(l, at, 1, c)
                    hT_upper(c - 1)
                    hi(l, at, 2, c)
                    tanh(c)
                next_hi(l, f, at, 0)
                hT_upper(CHUNKS - 1)
                next_hi(l, f, at, 1)

            def mixer(l):
                ph = l * PHASES + 1
                input_begin(ph)
                input_end(l, ph, M_AT)
                for m in range(M_UNITS):
                    if m > 0:
                        hi(l, M_AT, m + 2)
                    if m == 1:
                        act.wait_ge(rstd_ready, ph + 1)
                    i, _ = step_chunk(m - 1)
                    if i is not None and chunk_steps(i)[-1] == m - 1:
                        if 1 <= i < GROUPS or i == 5:
                            act.wait_ge(rope_dve, l * GROUPS + min(i, GROUPS))
                            act.wait_ge(rope_pool, l * GROUPS + min(i, GROUPS))
                        if i == 6:
                            act.wait_ge(qkT_done, l * 5 + 4)
                        for t in range(TT):
                            if t == 0:
                                act.wait_ge(proj_done, l * PROJ_CHUNKS + i + 1)
                            else:
                                unit_used(act, l, M_AT, m - 1)
                            src = bank[PROJ[i % 2][t]]
                            if i >= 8:
                                g0 = (i - 8) * NB
                                act.activation(gates[:, t, g0:g0 + NB], src[:, :], ACT.Tanh,
                                               scale=half_rstd[:, t:t + 1]).then_inc(gates_done, 1)
                                continue
                            w = NB
                            if i in (3, 4, 7):
                                v0 = {3: 0, 4: NB, 7: DIL_W}[i]
                                w = DIL_W - NB if i == 4 else NB
                                dst = v[:, t, v0:v0 + w]
                            else:
                                dst = qk_raw[:, t, :]
                            act.activation(dst, src[:, 0:w], ACT.Copy, scale=rstd[:, t:t + 1]).then_inc(proj_read, 1)
                    p = step_pair(m)
                    if p is not None:
                        for hh in range(2):
                            h = 2 * p + hh
                            act.wait_ge(neg_top_done, l * HEADS + h + 1)
                            for t in range(TT):
                                part = probs[:, hh, t, 0:keys(h)]
                                e = act.activation(part, part, ACT.Exp,
                                                   bias=neg_top[:, h, t:t + 1], accum_out=den[:, h, t:t + 1])
                            e.then_inc(exp_done, 1)
                    for j, i in enumerate(QK_CHUNKS):
                        if m == chunk_steps(i)[-1] + 2:
                            act.wait_ge(qkT_done, l * 5 + j + 1)
                            for s in range(2):
                                ft = bank[PROJ[i % 2][s]][:, :].rearrange("p (f s) -> p f s", f=2)
                                if i < GROUPS:
                                    dst = (qT, kT)[s][:, 2 * i:2 * i + 2, :]
                                else:
                                    at = DIL_PAIRS + 2 * s
                                    dst = (qT, kT)[i - 5][:, at:at + 2, :]
                                is_q = (i < GROUPS and s == 0) or i == 5
                                if i == 5:
                                    dst = dst.rearrange("p f (j r) -> p f r j", r=STRIDE)
                                    ft = ft.rearrange("p f (r j) -> p f r j", r=STRIDE)
                                act.activation(dst, ft, ACT.Copy, scale=HD ** -0.5 if is_q else 1.0).then_inc(qkT_read, 1)
                    if m == pair_step(DIL_PAIRS - 1) + 1:
                        act.wait_ge(mix_exp_in, l + 1)
                        act.activation(mix_e[:, :, :], mix_d[:, :, :], ACT.Exp).then_inc(mix_exp, 1)
                    if m == Y_AT:
                        for j in range(3):
                            act.wait_ge(yT_done, l * 3 + j + 1)
                            dst, src = yT_parts(yT_hi, j)
                            act.activation(dst, src, ACT.Copy).then_inc(yT_hi_done, 1)
                    if m == O_AT - 1:
                        for g, (t, n) in enumerate(GROUP4):
                            act.wait_ge(mT_done, l * 4 + g + 1)
                            act.activation(a_hi[:, 4 * n:4 * n + 4, t * P:(t + 1) * P],
                                           bank[MT[g % 2]][:, :].rearrange("p (k s) -> p k s", k=4),
                                           ACT.Copy).then_inc(mT_hi, 1)

            transposed_hi(0, 0)
            act.wait_ge(raw_arrived[0], 32)
            act.activation(w_hi[0][:, 0:D], raw[0][:, 0:D], ACT.Copy).then_inc(first_half, 1)
            act.activation(w_hi[0][:, D:UNIT], raw[0][:, D:UNIT], ACT.Copy).then_inc(hi_done, 1)
            transposed_hi(0, 1)
            act.dma_start(cst[:, 0:C_IDENT], consts[:, 0:C_IDENT]).then_inc(consts_loaded, 16)
            hi(0, F1_AT, 1)
            for t in range(TT):
                act.wait_ge(x_loaded[t], 16 * P // RUN)
                sum_squares(0, t)
            sum_squares(0, 2)
            with act.Fori(0, DEPTH) as l:
                feed_forward(l, 0, F1_AT)
                mixer(l)
                feed_forward(l, 1, F2_AT)
                ph = l * PHASES + PHASES
                sum_squares(ph, 0)
                with act.If(DEPTH - 1 - l):
                    transposed_hi(ph, 0)
                sum_squares(ph, 1)
                sum_squares(ph, 2)
                with act.If(DEPTH - 1 - l):
                    transposed_hi(ph, 1)
            sum_squares(DEPTH * PHASES, 3, last=True)

        @block.vector
        def _(dve):
            for i in range(2 * RING):
                dve.memset(credits[:, i:i + 1], 0.0).then_inc((lo_done, split_free)[i % 2], 1)

            def lo(l, at, u, c=None):
                slot = (at + u) % RING
                n = l * L_UNITS + at + u
                if c is not None:
                    n = n + c * 3
                dve.wait_ge(hi_done, n + 1)
                dve.tensor_tensor(w_lo[slot][:, :], raw[slot][:, :], w_hi[slot][:, :].bitcast(F32),
                                  ALU.subtract).then_inc(lo_done, 1)

            def update(l, ph, end, g):
                t, n = GROUP4[g]
                k = (ph - 1) * 4 + g + 1
                if g < 3:
                    dve.wait_ge(acc_done, (ph - 1) * 3 + g + 1)
                else:
                    unit_used(dve, l, end, -1)
                part = x[:, t, n * NB:(n + 1) * NB]
                dve.scalar_tensor_tensor(part, bank[ACC[t][n]][:, :], 0.5, part, ALU.mult, ALU.add).then_inc(x_updated, 1)
                return k

            def scaled(ph, g, updated=None):
                t, n = GROUP4[g]
                if updated is not None:
                    dve.wait_ge(x_updated, updated)
                dve.tensor_tensor(xg[:, t, n * NB:(n + 1) * NB], x[:, t, n * NB:(n + 1) * NB],
                                  gain[:, n * NB:(n + 1) * NB], ALU.mult).then_inc(xg_ready, 1)

            def transposed_lo(ph, g):
                t, n = GROUP4[g]
                dve.wait_ge(xT_hi, ph * 4 + g + 1)
                dve.tensor_tensor(a_lo[:, 4 * n:4 * n + 4, t * P:(t + 1) * P],
                                  bank[TR[g % 2]][:, :].rearrange("p (k s) -> p k s", k=4),
                                  a_hi[:, 4 * n:4 * n + 4, t * P:(t + 1) * P].bitcast(F32),
                                  ALU.subtract).then_inc(xT_lo, 1)

            def input_groups(l, ph, at):
                dve.wait_ge(gain_loaded, ph * 16 + 16)
                for g in range(3):
                    scaled(ph, g, update(l, ph, at, g))
                transposed_lo(ph, 0)
                scaled(ph, 3, update(l, ph, at, 3))
                transposed_lo(ph, 1)
                lo(l, at, 1)

            def end_groups(l):
                ph = l * PHASES + PHASES
                dve.wait_ge(gain_loaded, ph * 16 + 16)
                for g in range(3):
                    scaled(ph, g, update(l, ph, L_UNITS, g))
                with dve.If(DEPTH - 1 - l):
                    transposed_lo(ph, 0)
                scaled(ph, 3, update(l, ph, L_UNITS, 3))
                with dve.If(DEPTH - 1 - l):
                    transposed_lo(ph, 1)
                    lo(l, L_UNITS, 1)

            def input_end(l, ph, at):
                transposed_lo(ph, 2)
                lo(l, at, 2)
                transposed_lo(ph, 3)

            def next_lo(l, f, at):
                if f == 0:
                    lo(l, at, F_UNITS)
                else:
                    with dve.If(DEPTH - 1 - l):
                        lo(l, at, F_UNITS)

            def feed_forward(l, f, at):
                ph = l * PHASES + 2 * f
                ff = l * 2 + f
                if f == 1:
                    input_groups(l, ph, at)
                input_end(l, ph, at)
                dve.wait_ge(rstd_ready, ph + 1)

                def hide(c):
                    for t in range(TT):
                        k = ff * 2 * CHUNKS + c * 2 + t + 1
                        dve.wait_ge(tanh_done, k)
                        dve.scalar_tensor_tensor(gated[:, t, :], tanh_g[:, t, :], 1.0, bank[UP[t]][:, 0:FC],
                                                 ALU.add, ALU.mult).then_inc(gated_done, 1)
                        dve.wait_ge(gated_done, k)
                        dve.scalar_tensor_tensor(hidden[:, t, :], gated[:, t, :], half_rstd2[:, t:t + 1],
                                                 bank[UP[t]][:, FC:2 * FC], ALU.mult, ALU.mult).then_inc(hidden_done, 1)

                def hT_lower(c):
                    for t in range(TT):
                        toks = slice(t * P, (t + 1) * P)
                        dve.wait_ge(hT_hi_done, ff * 2 * CHUNKS + c * 2 + t + 1)
                        dve.tensor_tensor(hT_lo[:, :, toks], bank[HT[t]][:, 0:2 * P].rearrange("p (k s) -> p k s", k=2),
                                          hT_hi[:, :, toks].bitcast(F32), ALU.subtract).then_inc(hT_lo_done, 1)

                hide(0)
                with dve.Fori(1, CHUNKS) as c:
                    lo(l, at, 0, c)
                    lo(l, at, 1, c)
                    hT_lower(c - 1)
                    lo(l, at, 2, c)
                    hide(c)
                next_lo(l, f, at)
                hT_lower(CHUNKS - 1)

            def rope(l, i):
                heads = qk_raw[:, :, :].rearrange("p t (h s d) -> p t h s d", h=8, s=2)
                turned = qk_rot.rearrange("p t (h s d) -> p t h s d", h=8, s=2)
                c = cos.unsqueeze(2).to_broadcast([P, TT, 8, HALF])
                s = sin.unsqueeze(2).to_broadcast([P, TT, 8, HALF])
                dve.wait_ge(proj_read, l * 16 + 2 * i + 2)
                if i >= 1:
                    dve.wait_ge(qkT_done, l * 5 + i)
                dve.tensor_tensor(rope_tmp[:, 0], heads[:, :, :, 0, :], c, ALU.mult).then_inc(rope_dve_part, 1)
                dve.tensor_tensor(rope_tmp[:, 1], heads[:, :, :, 1, :], s, ALU.mult).then_inc(rope_dve_part, 1)
                dve.wait_ge(rope_dve_part, l * 6 + 2 * i + 2)
                dve.tensor_tensor(turned[:, :, :, 0, :], rope_tmp[:, 0], rope_tmp[:, 1], ALU.subtract).then_inc(rope_dve, 1)

            def probs_turned(l, h):
                dve.wait_ge(probsT_done, l * HEADS + h + 1)
                if h >= 2:
                    dve.wait_ge(pv_done, l * HEADS + h - 1)
                kts = keys(h) // P
                dve.tensor_copy(probsT[:, h % 2, 0:kts, :],
                                bank[PT][:, 0:kts * SEQ].rearrange("p (k q) -> p k q", k=kts)).then_inc(probsT_read, 1)

            def masked(l, h):
                hh = h % 2
                dve.wait_ge(scores_done, l * HEADS + h + 1)
                if h >= 2:
                    dve.wait_ge(probsT_done, l * HEADS + h - 1)
                dve.memset(wait_carrier[:, :], 0.0)
                for t in range(TT):
                    sc = bank[SC[hh]][:, t * SEQ:t * SEQ + keys(h)]
                    to = probs[:, hh, t, 0:keys(h)]
                    if h < GROUP_HEADS:
                        more = near_mask[:, t, :]
                    elif h < DIL_HEADS:
                        more = block_mask[:, h // GROUP_HEADS - 1, :]
                    else:
                        more = bias[:, h - DIL_HEADS, 2 - 2 * t:6 - 2 * t, :].rearrange("p g (j r) -> p r (g j)", r=STRIDE)
                        sc = sc.rearrange("p (r j) -> p r j", r=STRIDE)
                        to = to.rearrange("p (r j) -> p r j", r=STRIDE)
                    r = dve.tensor_tensor_reduce(to, sc, more, 1.0, -3.0e38, ALU.add, ALU.max, top[:, h, t:t + 1])
                r.then_inc(scores_read, 1)
                dve.wait_ge(scores_read, l * HEADS + h + 1)
                dve.tensor_scalar(neg_top[:, h, :], top[:, h, :], -1.0, None, ALU.mult).then_inc(neg_top_done, 1)

            def products_read(l, p):
                src = bank[OB][:, 0:2 * TT * HD].rearrange("p (h t d) -> p h t d", h=2, t=TT)
                if p < DIL_PAIRS:
                    dve.wait_ge(pv_done, l * HEADS + 2 * p + 2)
                    dve.tensor_copy(o_dil[:, 2 * p:2 * p + 2, :, :], src).then_inc(o_read, 1)
                    return
                j = p - DIL_PAIRS
                dve.reciprocal(rden[:, :, :], den[:, 2 * p:2 * p + 2, :]).then_inc(rden_done, 1)
                dve.wait_ge(rden_done, l * (PAIRS - DIL_PAIRS) + j + 1)
                dve.wait_ge(pv_done, l * HEADS + 2 * p + 2)
                at = GROUP_HEADS * HD + 2 * j * HD
                dst = y[:, :, at:at + 2 * HD].rearrange("p t (h d) -> p h t d", h=2)
                dve.tensor_tensor(dst, src, rden[:, :, :].unsqueeze(3).to_broadcast([P, 2, TT, HD]),
                                  ALU.mult).then_inc(o_read, 1)

            def mix_weights(l):
                n = [0]
                tops = top[:, 0:DIL_HEADS, :].rearrange("p (g h) t -> p g (h t)", g=GROUPS)
                dens = den[:, 0:DIL_HEADS, :].rearrange("p (g h) t -> p g (h t)", g=GROUPS)

                def chained(ins):
                    ins.then_inc(mix_chain, 1)
                    n[0] += 1
                    dve.wait_ge(mix_chain, l * 6 + n[0])
                peak = mix[:, 1, :]
                chained(dve.tensor_tensor(mix[:, 0, :], tops[:, 0, :], tops[:, 1, :], ALU.max))
                chained(dve.tensor_tensor(peak, mix[:, 0, :], tops[:, 2, :], ALU.max))
                dve.tensor_tensor(mix_d[:, :, :], tops, peak.unsqueeze(1).to_broadcast([P, GROUPS, GROUP_HEADS * TT]),
                                  ALU.subtract).then_inc(mix_exp_in, 1)
                dve.wait_ge(mix_exp, l + 1)
                chained(dve.tensor_tensor(mix_d[:, :, :], mix_e[:, :, :], dens, ALU.mult))
                chained(dve.tensor_tensor(mix[:, 2, :], mix_d[:, 0, :], mix_d[:, 1, :], ALU.add))
                chained(dve.tensor_tensor(mix[:, 3, :], mix[:, 2, :], mix_d[:, 2, :], ALU.add))
                chained(dve.reciprocal(mix[:, 4, :], mix[:, 3, :]))
                dve.tensor_tensor(mix_d[:, :, :], mix_e[:, :, :],
                                  mix[:, 4, :].unsqueeze(1).to_broadcast([P, GROUPS, GROUP_HEADS * TT]),
                                  ALU.mult).then_inc(mix_ready, 1)

            def merge(l):
                dve.wait_ge(a_read, l * 4 + 4)
                for g, (t, n) in enumerate(GROUP4):
                    if g < 3:
                        dve.wait_ge(b_done, l * 3 + g + 1)
                    else:
                        unit_used(dve, l, M_AT, O_AT - 1)
                    if g >= 1:
                        dve.wait_ge(merged_done, l * 4 + g)
                    dve.scalar_tensor_tensor(from_b, gates[:, t, D + n * NB:D + (n + 1) * NB], 1.0,
                                             bank[BANK_B[t][n]][:, :], ALU.add, ALU.mult).then_inc(b_read, 1)
                    if g >= 2:
                        merged_lo(l, g - 2)
                    dve.wait_ge(b_read, l * 4 + g + 1)
                    part = merged[:, t, n * NB:(n + 1) * NB]
                    dve.tensor_tensor(part, part, from_b, ALU.add).then_inc(merged_done, 1)

            def mixer(l):
                ph = l * PHASES + 1
                input_groups(l, ph, M_AT)
                input_end(l, ph, M_AT)
                dve.wait_ge(consts_loaded, 16)
                for m in range(M_UNITS):
                    p = step_pair(m)
                    before = step_pair(m - 1)
                    for hh in range(2):
                        if before is not None:
                            probs_turned(l, 2 * before + hh)
                        if p is not None:
                            if p == DIL_PAIRS and hh == 0:
                                dve.wait_ge(bias_ready, l + 1)
                            masked(l, 2 * p + hh)
                    if m == O_AT - 1:
                        merge(l)
                    if 0 < m < M_UNITS - 1:
                        lo(l, M_AT, m + 2)
                    if m == O_AT - 1:
                        merged_lo(l, 2)
                        merged_lo(l, 3)
                    if m in (2, 4, 6):
                        rope(l, m // 2 - 1)
                    if before is not None:
                        products_read(l, before)
                    if before == DIL_PAIRS - 1:
                        mix_weights(l)
                    if m == Y_AT:
                        for j in range(3):
                            dve.wait_ge(yT_hi_done, l * 3 + j + 1)
                            dst, src = yT_parts(yT_lo, j)
                            upper, _ = yT_parts(yT_hi, j)
                            dve.tensor_tensor(dst, src, upper.bitcast(F32), ALU.subtract).then_inc(yT_lo_done, 1)
                    if m == BA_AT:
                        dve.wait_ge(gates_done, l * 8 + 8)
                        for g, (t, n) in enumerate(GROUP4):
                            if g < 3:
                                dve.wait_ge(a_done, l * 3 + g + 1)
                            else:
                                unit_used(dve, l, M_AT, BA_AT)
                            dve.scalar_tensor_tensor(merged[:, t, n * NB:(n + 1) * NB], gates[:, t, n * NB:(n + 1) * NB], 1.0,
                                                     bank[BANK_A[t][n]][:, :], ALU.add, ALU.mult).then_inc(a_read, 1)
            def merged_lo(l, g):
                t, n = GROUP4[g]
                dve.wait_ge(mT_hi, l * 4 + g + 1)
                dve.tensor_tensor(a_lo[:, 4 * n:4 * n + 4, t * P:(t + 1) * P],
                                  bank[MT[g % 2]][:, :].rearrange("p (k s) -> p k s", k=4),
                                  a_hi[:, 4 * n:4 * n + 4, t * P:(t + 1) * P].bitcast(F32),
                                  ALU.subtract).then_inc(mT_lo, 1)

            dve.wait_ge(first_gain, 16)
            dve.wait_ge(x_loaded[0], 16 * P // RUN)
            scaled(0, 0)
            transposed_lo(0, 0)
            dve.wait_ge(x_loaded[1], 16 * P // RUN)
            scaled(0, 1)
            dve.wait_ge(first_half, 1)
            dve.tensor_tensor(w_lo[0][:, 0:D], raw[0][:, 0:D], w_hi[0][:, 0:D].bitcast(F32), ALU.subtract)
            dve.wait_ge(hi_done, 1)
            dve.tensor_tensor(w_lo[0][:, D:UNIT], raw[0][:, D:UNIT], w_hi[0][:, D:UNIT].bitcast(F32),
                              ALU.subtract).then_inc(lo_done, 1)
            transposed_lo(0, 1)
            dve.wait_ge(gain_loaded, 16)
            scaled(0, 2)
            scaled(0, 3)
            lo(0, F1_AT, 1)
            with dve.Fori(0, DEPTH) as l:
                feed_forward(l, 0, F1_AT)
                mixer(l)
                feed_forward(l, 1, F2_AT)
                end_groups(l)
            dve.wait_ge(rstd_ready, DEPTH * PHASES + 1)
            for t in range(TT):
                dve.wait_ge(xg_ready, DEPTH * PHASES * 4 + t + 3)
                dve.tensor_scalar(xg[:, t, :], xg[:, t, :], rstd[:, t:t + 1], None, ALU.mult).then_inc(result_ready, 1)

        @block.tensor
        def _(pe):
            def product(dst, s_hi, s_lo, m_hi, m_lo, start, stop):
                pe.matmul(dst, s_hi, m_hi, start=start, stop=False)
                pe.matmul(dst, s_hi, m_lo, start=False, stop=False)
                return pe.matmul(dst, s_lo, m_hi, start=False, stop=stop)

            def split_ready(l, at, u, c=None):
                n = l * L_UNITS + at + u
                if c is not None:
                    n = n + c * 3
                pe.wait_ge(lo_done, n + 1 + RING)

            def cols(slot, t, a, dst, start, stop, js=range(4), nk=4):
                w = UNIT // nk
                for j in js:
                    k = nk * a + j
                    mm = product(dst[:, 0:w], a_hi[:, k, t * P:(t + 1) * P], a_lo[:, k, t * P:(t + 1) * P],
                                 w_hi[slot][:, j * w:(j + 1) * w], w_lo[slot][:, j * w:(j + 1) * w],
                                 start and j == 0, stop and j == nk - 1)
                return mm

            def rows(slot, s_hi, s_lo, k0, t, n, dst, start, stop):
                for j in range(2):
                    at = j * D + n * NB
                    mm = product(dst[:, :], s_hi[:, k0 + j, t * P:(t + 1) * P], s_lo[:, k0 + j, t * P:(t + 1) * P],
                                 w_hi[slot][:, at:at + NB], w_lo[slot][:, at:at + NB], start and j == 0, stop and j == 1)
                return mm

            def input_transposes(ph, g):
                t, n = GROUP4[g]
                pe.wait_ge(xg_ready, ph * 4 + g + 1)
                if g >= 2:
                    pe.wait_ge(xT_lo, ph * 4 + g - 1)
                for j in range(4):
                    c = n * NB + j * P
                    tr = pe.transpose(bank[TR[g % 2]][:, j * P:(j + 1) * P], xg[:, t, c:c + P], ident)
                tr.then_inc(xT_done, 1)

            def input_products(l, ph, at, part):
                input_transposes(ph, 1)
                for a in range(2):
                    split_ready(l, at, a)
                    for t in range(TT):
                        pe.wait_ge(xT_lo, ph * 4 + 2 * a + t + 1)
                        part(a, t)
                        if a == 0:
                            input_transposes(ph, t + 2)

            def feed_forward(l, f, at):
                ph = l * PHASES + 2 * f
                ff = l * 2 + f

                def up(c, a, t, slot):
                    mm = cols(slot, t, a, bank[UP[t]], a == 0, a == 1)
                    if t == 1:
                        mm.then_inc(split_free, 1)
                    elif a == 1:
                        mm.then_inc(up_done, 1)

                def turn(c, t):
                    pe.wait_ge(hidden_done, ff * 2 * CHUNKS + c * 2 + t + 1)
                    for j in range(2):
                        tr = pe.transpose(bank[HT[t]][:, j * P:(j + 1) * P], hidden[:, t, j * P:(j + 1) * P], ident)
                    tr.then_inc(hT_done, 1)

                def down(c, slot, start, stop, between=None):
                    for g, (t, n) in enumerate(GROUP4):
                        if n == 0:
                            pe.wait_ge(hT_lo_done, ff * 2 * CHUNKS + c * 2 + t + 1)
                        if g == 3 and between is not None:
                            between()
                        mm = rows(slot, hT_hi, hT_lo, 0, t, n, bank[ACC[t][n]], start, stop)
                        if g == 3:
                            mm.then_inc(split_free, 1)
                        elif stop:
                            mm.then_inc(acc_done, 1)

                input_products(l, ph, at, lambda a, t: up(0, a, t, a))

                def chunk(c, first, last):
                    split_ready(l, at, -1, c)
                    for t in range(TT):
                        pe.wait_ge(hidden_done, ff * 2 * CHUNKS + (c - 1) * 2 + t + 1)
                        up(c, 0, t, 2)
                    for t in range(TT):
                        turn(c - 1, t)
                    split_ready(l, at, 0, c)
                    for t in range(TT):
                        up(c, 1, t, 0)
                    split_ready(l, at, 1, c)
                    down(c - 1, 1, first, False, (lambda: turn(c, 0)) if last else None)

                chunk(1, True, False)
                with pe.Fori(2, CHUNKS - 1) as c:
                    chunk(c, False, False)
                chunk(CHUNKS - 1, False, True)
                turn(CHUNKS - 1, 1)
                split_ready(l, at, F_UNITS - 1)
                down(CHUNKS - 1, 2, False, True, lambda: next_transposes(l, f, ph + 1))

            def next_transposes(l, f, ph):
                if f == 0:
                    input_transposes(ph, 0)
                else:
                    with pe.If(DEPTH - 1 - l):
                        input_transposes(ph, 0)

            def qk_transposes(l, j, i):
                if i < GROUPS:
                    pe.wait_ge(rope_dve, l * GROUPS + i + 1)
                    pe.wait_ge(rope_pool, l * GROUPS + i + 1)
                    src = qk_rot
                else:
                    pe.wait_ge(proj_read, l * 16 + 2 * i + 2)
                    src = qk_raw
                for f in range(4):
                    for t in range(TT):
                        at = (f % 2) * SEQ + t * P
                        tr = pe.transpose(bank[PROJ[i % 2][f // 2]][:, at:at + P], src[:, t, f * P:(f + 1) * P], ident)
                tr.then_inc(qkT_done, 1)

            def scores(l, p):
                for t in range(TT):
                    for hh in range(2):
                        h = 2 * p + hh
                        rows_ = slice(hh * HD, (hh + 1) * HD)
                        k0 = t * P if keys(h) == P else 0
                        mm = pe.matmul(bank[SC[hh]][:, t * SEQ:t * SEQ + keys(h)], qT[rows_, p, t * P:(t + 1) * P],
                                       kT[rows_, p, k0:k0 + keys(h)], start=True, stop=True)
                        if t == TT - 1:
                            mm.then_inc(scores_done, 1)

            def turn_probs(l, h):
                pe.wait_ge(exp_done, l * HEADS + h + 1)
                if h >= 1:
                    pe.wait_ge(probsT_read, l * HEADS + h)
                for k in range(keys(h) // P):
                    for t in range(TT):
                        part = probs[:, h % 2, t, k * P:(k + 1) * P]
                        tr = pe.transpose(bank[PT][:, k * SEQ + t * P:k * SEQ + (t + 1) * P], part, ident)
                tr.then_inc(probsT_done, 1)

            def times_v(l, h):
                p, hh = h // 2, h % 2
                pe.wait_ge(probsT_read, l * HEADS + h + 1)
                if hh == 0:
                    if p >= 1:
                        pe.wait_ge(o_read, l * PAIRS + p)
                    pe.wait_ge(proj_read, l * 16 + (10 if p < DIL_PAIRS else 16))
                for t in range(TT):
                    kts = range(TT) if keys(h) == SEQ else (t,)
                    for k in kts:
                        at = (hh * TT + t) * HD
                        mm = pe.matmul(bank[OB][:, at:at + HD], probsT[:, hh, k - kts[0], t * P:(t + 1) * P],
                                       v[:, k, h * HD:(h + 1) * HD], start=k == kts[0], stop=k == kts[-1])
                mm.then_inc(pv_done, 1)

            def mixer(l):
                ph = l * PHASES + 1
                def first_chunk(a, t):
                    mm = cols((M_AT + a) % RING, t, a, bank[PROJ[0][t]], a == 0, a == 1)
                    if t == 1:
                        mm.then_inc(split_free, 1)
                    elif a == 1:
                        mm.then_inc(proj_done, 1)

                def merged_transposes(g):
                    t, n = GROUP4[g]
                    pe.wait_ge(merged_done, l * 4 + g + 1)
                    if g >= 2:
                        pe.wait_ge(mT_lo, l * 4 + g - 1)
                    for j in range(4):
                        c = n * NB + j * P
                        tr = pe.transpose(bank[MT[g % 2]][:, j * P:(j + 1) * P], merged[:, t, c:c + P], ident)
                    tr.then_inc(mT_done, 1)

                input_products(l, ph, M_AT, first_chunk)
                for m in range(2, O_AT):
                    slot = (M_AT + m) % RING
                    p, before = step_pair(m), step_pair(m - 1)
                    if before is not None:
                        turn_probs(l, 2 * before)
                    if p is not None:
                        pe.wait_ge(qkT_read, l * 10 + (2 * (p // 2) + 2 if p < DIL_PAIRS else 10))
                        if p >= 1:
                            pe.wait_ge(scores_read, l * HEADS + 2 * p)
                        scores(l, p)
                    if m == Y_AT:
                        pe.wait_ge(y_dil_done, l + 1)
                        pe.wait_ge(o_read, l * PAIRS + PAIRS)
                        for j in range(3):
                            for f in range(2):
                                for t in range(TT):
                                    at = f * SEQ + t * P
                                    c = (2 * j + f) * P
                                    tr = pe.transpose(bank[YT[j]][:, at:at + P], y[:, t, c:c + P], ident)
                            tr.then_inc(yT_done, 1)
                    i, a = step_chunk(m)
                    if i is not None:
                        if a == 0 and i >= 2:
                            if i - 2 in QK_CHUNKS:
                                pe.wait_ge(qkT_read, l * 10 + 2 * QK_CHUNKS.index(i - 2) + 2)
                            elif i - 2 < 8:
                                pe.wait_ge(proj_read, l * 16 + 2 * (i - 2) + 2)
                            else:
                                pe.wait_ge(gates_done, l * 8 + 2 * (i - 10) + 2)
                        split_ready(l, M_AT, m)
                        last = a == len(chunk_steps(i)) - 1
                        nk = 8 if i == 4 else 4
                        for t in range(TT):
                            if t == 1:
                                for j, turned in enumerate(QK_CHUNKS):
                                    if m == chunk_steps(turned)[-1] + 2:
                                        qk_transposes(l, j, turned)
                            for q in range(2):
                                js = range(q * nk // 2, (q + 1) * nk // 2)
                                mm = cols(slot, t, a, bank[PROJ[i % 2][t]], a == 0, last, js, nk)
                                if q == 1 and t == 1:
                                    mm.then_inc(split_free, 1)
                                elif q == 1 and last:
                                    mm.then_inc(proj_done, 1)
                                if before is not None:
                                    if t == 0 and q == 0:
                                        turn_probs(l, 2 * before + 1)
                                    if t == 0 and q == 1:
                                        times_v(l, 2 * before)
                                    if t == 1 and q == 0:
                                        times_v(l, 2 * before + 1)
                    elif m == BA_AT:
                        split_ready(l, M_AT, m)
                        pe.wait_ge(yT_lo_done, l * 3 + 3)
                        pe.wait_ge(gates_done, l * 8 + 6)
                        for g, (t, n) in enumerate(GROUP4):
                            mm = rows(slot, yT_hi, yT_lo, 0, t, n, bank[BANK_A[t][n]], True, True)
                            mm.then_inc(a_done if g < 3 else split_free, 1)
                    else:
                        split_ready(l, M_AT, m)
                        if m == BB_AT:
                            pe.wait_ge(gates_done, l * 8 + 8)
                        last = m == BB_AT + 1
                        for g, (t, n) in enumerate(GROUP4):
                            if last and g == 3:
                                merged_transposes(0)
                            mm = rows(slot, yT_hi, yT_lo, 2 * (m - BB_AT) + 2, t, n, bank[BANK_B[t][n]], not last, last)
                            if g == 3:
                                mm.then_inc(split_free, 1)
                            elif last:
                                mm.then_inc(b_done, 1)

                merged_transposes(1)
                for j in range(4):
                    m = O_AT + j
                    split_ready(l, M_AT, m)
                    if j == 2:
                        pe.wait_ge(mT_lo, l * 4 + 4)
                    for g, (t, n) in enumerate(GROUP4):
                        if j == 0 and n == 0:
                            pe.wait_ge(mT_lo, l * 4 + t + 1)
                        if j == 3 and g == 3:
                            input_transposes(ph + 1, 0)
                        mm = rows((M_AT + m) % RING, a_hi, a_lo, 2 * j, t, n, bank[ACC[t][n]], j == 0, j == 3)
                        if g == 3:
                            mm.then_inc(split_free, 1)
                        elif j == 3:
                            mm.then_inc(acc_done, 1)
                    if j == 0:
                        merged_transposes(2)
                        merged_transposes(3)

            pe.wait_ge(ident_loaded, 16)
            input_transposes(0, 0)
            with pe.Fori(0, DEPTH) as l:
                feed_forward(l, 0, F1_AT)
                mixer(l)
                feed_forward(l, 1, F2_AT)


_INS = ["ffn1_w_up", "ffn1_w_down", "ffn2_w_up", "ffn2_w_down", "w_in", "na_rel_bias", "w_branch_a", "w_branch_b", "w_out"]


def _constants():
    pos = np.arange(SEQ).reshape(RUN, STRIDE).T.reshape(-1)
    rel = pos[None, :] - pos[:, None]
    parts = []
    for g, (window, dilation) in enumerate(DIL_PATTERNS):
        half = window // 2 // dilation
        ok = (rel % dilation == 0) & (np.abs(rel) <= half * dilation)
        mask = np.where(ok, 0.0, NEG_INF).astype(np.float32)
        if g == 0:
            parts += [mask[t * P:(t + 1) * P] for t in range(TT)]
        else:
            assert mask[:P, P:].max() == mask[P:, :P].max() == NEG_INF and (mask[:P, :P] == mask[P:, P:]).all()
            parts.append(mask[:P, :P])
    qc = np.arange(P) % GRID_W
    low = np.clip(qc - NA_COLS // 2, 0, GRID_W - NA_COLS)[:, None]
    kc = np.arange(GRID_W)[None, :]
    parts.append(np.where((kc >= low) & (kc < low + NA_COLS), 0.0, NEG_INF).astype(np.float32))
    freq = np.float32(10000.0) ** (-np.arange(HALF, dtype=np.float32) / np.float32(HALF))
    angle = pos.astype(np.float32)[:, None] * freq[None, :]
    for table in (np.cos(angle), np.sin(angle)):
        parts += [table[t * P:(t + 1) * P].astype(np.float32) for t in range(TT)]
    parts.append(np.eye(P, dtype=np.float32))
    return np.concatenate(parts, axis=1)


def kernel(**inputs):
    import concourse.bacc as _bacc
    from concourse.bass_utils import run_bass_kernel_spmd as _run

    nc = _bacc.Bacc("TRN2", target_bir_lowering=False, num_devices=1)
    rows = [inputs[name][l] for l in range(DEPTH) for name in ("ffn1_norm", "mix_norm", "ffn2_norm")]
    arrays = {name: np.ascontiguousarray(inputs[name]) for name in _INS}
    arrays["x"] = np.ascontiguousarray(inputs["x"]).reshape(SEQ, D)
    arrays["gains"] = np.stack(rows + [inputs["final_norm"]])
    arrays["consts"] = _constants()
    ap = {name: nc.dram_tensor(f"{name}_dram", a.shape, F32, kind="ExternalInput").ap() for name, a in arrays.items()}
    out = nc.dram_tensor("out_dram", (SEQ, D), F32, kind="ExternalOutput").ap()
    build(nc, ap["x"], ap["gains"], (ap["ffn1_w_up"], ap["ffn2_w_up"]), (ap["ffn1_w_down"], ap["ffn2_w_down"]),
          ap["w_in"], ap["na_rel_bias"], ap["w_branch_a"], ap["w_branch_b"], ap["w_out"], ap["consts"], out)
    r = _run(nc, [{f"{name}_dram": a for name, a in arrays.items()}], core_ids=[0])
    return r.results[0]["out_dram"].reshape(1, SEQ, D)
```
